# Optimizing a Trainium2 kernel written in Bass

```python
import jax, jax.numpy as jnp
from jax import lax
import numpy as np

D_MODEL = 2048
BATCH = 1
SEQ = 256
DEPTH = 2
DEC_BATCH = 1
DEC_SEQ = 32
PAST_LEN = 128

CHUNK = 64
N_A_LAYERS = DEPTH // 2
N_B_LAYERS = DEPTH - N_A_LAYERS
RW_HEAD = 64
RW_HEADS = D_MODEL // RW_HEAD
RW_DECAY_LORA = 96
RW_AAA_LORA = 96
RW_MV_LORA = 64
RW_GATE_LORA = 256
GN_EPS = 64e-5
MLA_HEADS = 32
Q_RANK = 512
KV_RANK = 512
NOPE_DIM = 128
ROPE_DIM = 64
V_DIM = 128
ROPE_THETA = 10000.0
MLA_SCALE = (NOPE_DIM + ROPE_DIM) ** -0.5
D_FF = 4 * D_MODEL
Q_BLOCK = 128
NORM_EPS = 1e-6
N_MOD = 6

kernel_name = 'yoco_rwkv7_mla_stream_encoder'

def rmsnorm(x, g):
    xf = x.astype(jnp.float32)
    y = xf * lax.rsqrt(jnp.mean(xf * xf, axis=-1, keepdims=True) + NORM_EPS)
    return (y * g.astype(jnp.float32)).astype(x.dtype)

def modulate(h, shift, scale):
    return h * (1 + scale[:, None, :]) + shift[:, None, :]

def rope(x, pos):
    half = ROPE_DIM // 2
    inv = ROPE_THETA ** (-jnp.arange(half, dtype=jnp.float32) / half)
    ang = pos.astype(jnp.float32)[:, None] * inv[None, :]
    shape = (ang.shape[0],) + (1,) * (x.ndim - 3) + (half,)
    cos, sin = jnp.cos(ang).reshape(shape), jnp.sin(ang).reshape(shape)
    xf = x.astype(jnp.float32)
    x1, x2 = xf[..., :half], xf[..., half:]
    return jnp.concatenate([x1 * cos - x2 * sin, x2 * cos + x1 * sin], axis=-1).astype(x.dtype)

def rwkv7_time_mix(h, h_prev, s0, v_first, p, v_lora):
    B, T, D = h.shape
    xx = jnp.concatenate([h_prev[:, None, :].astype(h.dtype), h[:, :-1, :]], axis=1) - h
    mu = p['mu']
    r = (h + xx * mu[0]) @ p['wr']
    w = -jax.nn.softplus(-(p['w0'] + jnp.tanh((h + xx * mu[1]) @ p['w1']) @ p['w2'])) - 0.5
    k = (h + xx * mu[2]) @ p['wk']
    xv = h + xx * mu[3]
    v = xv @ p['wv']
    if v_lora is None:
        v_first = v
    else:
        v0, v1, v2 = v_lora
        v = v + (v_first - v) * jax.nn.sigmoid(v0 + (xv @ v1) @ v2)
    a = jax.nn.sigmoid(p['a0'] + ((h + xx * mu[4]) @ p['a1']) @ p['a2'])
    g = jax.nn.sigmoid((h + xx * mu[5]) @ p['g1']) @ p['g2']
    heads = lambda t: t.astype(jnp.float32).reshape(B, T, RW_HEADS, RW_HEAD)
    kk = heads(k * p['k_k'])
    kk = kk / jnp.maximum(jnp.sqrt(jnp.sum(kk * kk, axis=-1, keepdims=True)), 1e-12)
    k = k * (1 + (a - 1) * p['k_a'])
    decay = jnp.exp(-jnp.exp(heads(w)))
    tb = lambda t: jnp.swapaxes(t, 0, 1)
    xs = (tb(heads(r)), tb(decay), tb(heads(k)), tb(heads(v)), tb(kk), tb(kk * heads(a)))

    def step(S, inp):
        r_t, d_t, k_t, v_t, kk_t, b_t = inp
        sa = jnp.einsum('bhvk,bhk->bhv', S, kk_t)
        S = S * d_t[:, :, None, :] - sa[..., None] * b_t[:, :, None, :] + v_t[..., None] * k_t[:, :, None, :]
        return S, jnp.einsum('bhvk,bhk->bhv', S, r_t)

    s_fin, y = lax.scan(step, s0.astype(jnp.float32), xs)
    y = tb(y)
    mean = jnp.mean(y, -1, keepdims=True)
    var = jnp.mean(jnp.square(y - mean), -1, keepdims=True)
    yn = ((y - mean) * lax.rsqrt(var + GN_EPS)).reshape(B, T, D) * p['lnx_g'] + p['lnx_b']
    bonus = jnp.sum(heads(r * k * p['r_k']), -1, keepdims=True) * heads(v)
    out = ((yn + bonus.reshape(B, T, D)).astype(h.dtype) * g) @ p['wo']
    return out, v_first, s_fin, h[:, -1, :]

def sq_relu_mlp(h, w1, w2):
    return jnp.square(jax.nn.relu(h @ w1)) @ w2

def shared_latent(x, cs, pos, W):
    mod = cs @ W['kv_ada_w'] + W['kv_ada_b']
    h = modulate(rmsnorm(x, W['kv_norm_g']), mod[:, :D_MODEL], mod[:, D_MODEL:])
    kv = h @ W['kv_wd']
    ckv = rmsnorm(kv[..., :KV_RANK], W['kv_lat_g'])
    kpe = rope(kv[..., KV_RANK:], pos)
    return ckv, kpe

def mla_queries(h, pos, wdq, q_g, wuq):
    B, T, _ = h.shape
    cq = rmsnorm(h @ wdq, q_g)
    q = (cq @ wuq).reshape(B, T, MLA_HEADS, NOPE_DIM + ROPE_DIM)
    return q[..., :NOPE_DIM], rope(q[..., NOPE_DIM:], pos)

def latent_attention(q_nope, q_pe, q_pos, ckv, kpe, k_pos, w_uk, w_uv):
    q_lat = jnp.einsum('bqhd,chd->bqhc', q_nope, w_uk)
    s = jnp.einsum('bqhc,bkc->bhqk', q_lat, ckv) + jnp.einsum('bqhr,bkr->bhqk', q_pe, kpe)
    s = s.astype(jnp.float32) * MLA_SCALE
    visible = (k_pos[None, :] // CHUNK) <= (q_pos[:, None] // CHUNK)
    s = jnp.where(visible[None, None], s, -jnp.inf)
    pr = jax.nn.softmax(s, axis=-1).astype(ckv.dtype)
    o_lat = jnp.einsum('bhqk,bkc->bqhc', pr, ckv)
    return jnp.einsum('bqhc,chd->bqhd', o_lat, w_uv)

def prompt_attention(q_nope, q_pe, ckv, kpe, w_uk, w_uv):
    B, T = q_nope.shape[:2]
    nb = T // Q_BLOCK
    pos = jnp.arange(T)
    blocks = lambda t: jnp.moveaxis(t.reshape((B, nb, Q_BLOCK) + t.shape[2:]), 1, 0)

    def one(args):
        qn, qp, qpos = args
        return latent_attention(qn, qp, qpos, ckv, kpe, pos, w_uk, w_uv)

    o = lax.map(one, (blocks(q_nope), blocks(q_pe), pos.reshape(nb, Q_BLOCK)))
    return jnp.moveaxis(o, 0, 1).reshape(B, T, MLA_HEADS, V_DIM)

def trunk(x, c, pos, h_prev, s0, past_ckv, past_kpe, W):
    B, T, D = x.shape
    cs = jax.nn.silu(c)
    v_first = None
    shifts, states = [], []
    ckv = kpe = keys_ckv = keys_kpe = k_pos = None
    for l in range(DEPTH):
        mod = (cs @ W['ada_w'][l] + W['ada_b'][l]).reshape(B, N_MOD, D)
        h = modulate(rmsnorm(x, W['norm_mix_g'][l]), mod[:, 0], mod[:, 1])
        if l < N_A_LAYERS:
            p = dict(mu=W['rw_mu'][l], w0=W['rw_w0'][l], w1=W['rw_w1'][l], w2=W['rw_w2'][l],
                     a0=W['rw_a0'][l], a1=W['rw_a1'][l], a2=W['rw_a2'][l],
                     g1=W['rw_g1'][l], g2=W['rw_g2'][l], wr=W['rw_wr'][l], wk=W['rw_wk'][l],
                     wv=W['rw_wv'][l], wo=W['rw_wo'][l], k_k=W['rw_kk'][l], k_a=W['rw_ka'][l],
                     r_k=W['rw_rk'][l], lnx_g=W['rw_lnx_g'][l], lnx_b=W['rw_lnx_b'][l])
            v_lora = None if l == 0 else (W['rw_v0'][l - 1], W['rw_v1'][l - 1], W['rw_v2'][l - 1])
            out, v_first, s_fin, h_last = rwkv7_time_mix(h, h_prev[l], s0[l], v_first, p, v_lora)
            shifts.append(h_last)
            states.append(s_fin)
        else:
            j = l - N_A_LAYERS
            q_nope, q_pe = mla_queries(h, pos, W['mla_wdq'][j], W['mla_q_g'][j], W['mla_wuq'][j])
            if past_ckv is None:
                o = prompt_attention(q_nope, q_pe, ckv, kpe, W['kv_wuk'], W['kv_wuv'])
            else:
                o = latent_attention(q_nope, q_pe, pos, keys_ckv, keys_kpe, k_pos, W['kv_wuk'], W['kv_wuv'])
            out = o.reshape(B, T, MLA_HEADS * V_DIM) @ W['mla_wo'][j]
        x = x + mod[:, 2][:, None, :] * out
        h = modulate(rmsnorm(x, W['norm_mlp_g'][l]), mod[:, 3], mod[:, 4])
        x = x + mod[:, 5][:, None, :] * sq_relu_mlp(h, W['mlp_w1'][l], W['mlp_w2'][l])
        if l == N_A_LAYERS - 1:
            ckv, kpe = shared_latent(x, cs, pos, W)
            if past_ckv is not None:
                keys_ckv = jnp.concatenate([past_ckv.astype(ckv.dtype), ckv], axis=1)
                keys_kpe = jnp.concatenate([past_kpe.astype(kpe.dtype), kpe], axis=1)
                k_pos = jnp.arange(keys_ckv.shape[1])
    y = rmsnorm(x, W['final_g'])
    return y, ckv, kpe, jnp.stack(states), jnp.stack(shifts)

def setup_inputs(seed: int = 0) -> dict:
    key = jax.random.key(seed)
    ks = iter(jax.random.split(key, 64))

    def nrm(shape, scale=1.0, offset=0.0):
        return offset + scale * jax.random.normal(next(ks), shape, jnp.float32)

    D, NA, NB, H = D_MODEL, N_A_LAYERS, N_B_LAYERS, MLA_HEADS
    return {
        'x_prompt': nrm((BATCH, SEQ, D)),
        'x_sample': nrm((DEC_BATCH, DEC_SEQ, D)),
        'cache_ckv': nrm((DEC_BATCH, PAST_LEN, KV_RANK)),
        'cache_kpe': nrm((DEC_BATCH, PAST_LEN, ROPE_DIM)),
        'state_wkv': nrm((NA, DEC_BATCH, RW_HEADS, RW_HEAD, RW_HEAD), 0.3),
        'state_shift': nrm((NA, DEC_BATCH, D)),
        'c_prompt': nrm((BATCH, D)),
        'c_sample': nrm((DEC_BATCH, D)),
        'ada_w': nrm((DEPTH, D, N_MOD * D), 0.5 * D ** -0.5),
        'ada_b': nrm((DEPTH, N_MOD * D), 0.01),
        'norm_mix_g': nrm((DEPTH, D), 0.05, 1.0),
        'norm_mlp_g': nrm((DEPTH, D), 0.05, 1.0),
        'mlp_w1': nrm((DEPTH, D, D_FF), D ** -0.5),
        'mlp_w2': nrm((DEPTH, D_FF, D), D_FF ** -0.5),
        'rw_mu': nrm((NA, 6, D), 0.2, 0.5),
        'rw_w0': nrm((NA, D), 0.5, -2.0),
        'rw_w1': nrm((NA, D, RW_DECAY_LORA), D ** -0.5),
        'rw_w2': nrm((NA, RW_DECAY_LORA, D), 0.3 * RW_DECAY_LORA ** -0.5),
        'rw_a0': nrm((NA, D), 0.2),
        'rw_a1': nrm((NA, D, RW_AAA_LORA), D ** -0.5),
        'rw_a2': nrm((NA, RW_AAA_LORA, D), RW_AAA_LORA ** -0.5),
        'rw_v0': nrm((NA - 1, D), 0.2),
        'rw_v1': nrm((NA - 1, D, RW_MV_LORA), D ** -0.5),
        'rw_v2': nrm((NA - 1, RW_MV_LORA, D), RW_MV_LORA ** -0.5),
        'rw_g1': nrm((NA, D, RW_GATE_LORA), D ** -0.5),
        'rw_g2': nrm((NA, RW_GATE_LORA, D), RW_GATE_LORA ** -0.5),
        'rw_wr': nrm((NA, D, D), D ** -0.5),
        'rw_wk': nrm((NA, D, D), D ** -0.5),
        'rw_wv': nrm((NA, D, D), D ** -0.5),
        'rw_wo': nrm((NA, D, D), D ** -0.5),
        'rw_kk': nrm((NA, D), 0.05, 0.85),
        'rw_ka': nrm((NA, D), 0.05, 1.0),
        'rw_rk': nrm((NA, D), 0.1),
        'rw_lnx_g': nrm((NA, D), 0.05, 1.0),
        'rw_lnx_b': nrm((NA, D), 0.02),
        'kv_ada_w': nrm((D, 2 * D), 0.5 * D ** -0.5),
        'kv_ada_b': nrm((2 * D,), 0.01),
        'kv_norm_g': nrm((D,), 0.05, 1.0),
        'kv_wd': nrm((D, KV_RANK + ROPE_DIM), D ** -0.5),
        'kv_lat_g': nrm((KV_RANK,), 0.05, 1.0),
        'kv_wuk': nrm((KV_RANK, H, NOPE_DIM), KV_RANK ** -0.5),
        'kv_wuv': nrm((KV_RANK, H, V_DIM), KV_RANK ** -0.5),
        'mla_wdq': nrm((NB, D, Q_RANK), D ** -0.5),
        'mla_q_g': nrm((NB, Q_RANK), 0.05, 1.0),
        'mla_wuq': nrm((NB, Q_RANK, H * (NOPE_DIM + ROPE_DIM)), Q_RANK ** -0.5),
        'mla_wo': nrm((NB, H * V_DIM, D), (H * V_DIM) ** -0.5),
        'final_g': nrm((D,), 0.05, 1.0),
    }

def reference(x_prompt, x_sample, cache_ckv, cache_kpe, state_wkv, state_shift, c_prompt, c_sample,
              ada_w, ada_b, norm_mix_g, norm_mlp_g, mlp_w1, mlp_w2,
              rw_mu, rw_w0, rw_w1, rw_w2, rw_a0, rw_a1, rw_a2, rw_v0, rw_v1, rw_v2, rw_g1, rw_g2,
              rw_wr, rw_wk, rw_wv, rw_wo, rw_kk, rw_ka, rw_rk, rw_lnx_g, rw_lnx_b,
              kv_ada_w, kv_ada_b, kv_norm_g, kv_wd, kv_lat_g, kv_wuk, kv_wuv,
              mla_wdq, mla_q_g, mla_wuq, mla_wo, final_g):
    W = dict(ada_w=ada_w, ada_b=ada_b, norm_mix_g=norm_mix_g, norm_mlp_g=norm_mlp_g,
             mlp_w1=mlp_w1, mlp_w2=mlp_w2, rw_mu=rw_mu, rw_w0=rw_w0, rw_w1=rw_w1, rw_w2=rw_w2,
             rw_a0=rw_a0, rw_a1=rw_a1, rw_a2=rw_a2, rw_v0=rw_v0, rw_v1=rw_v1, rw_v2=rw_v2,
             rw_g1=rw_g1, rw_g2=rw_g2, rw_wr=rw_wr, rw_wk=rw_wk, rw_wv=rw_wv, rw_wo=rw_wo,
             rw_kk=rw_kk, rw_ka=rw_ka, rw_rk=rw_rk, rw_lnx_g=rw_lnx_g, rw_lnx_b=rw_lnx_b,
             kv_ada_w=kv_ada_w, kv_ada_b=kv_ada_b, kv_norm_g=kv_norm_g, kv_wd=kv_wd,
             kv_lat_g=kv_lat_g, kv_wuk=kv_wuk, kv_wuv=kv_wuv, mla_wdq=mla_wdq, mla_q_g=mla_q_g,
             mla_wuq=mla_wuq, mla_wo=mla_wo, final_g=final_g)
    Bp, Tp = x_prompt.shape[0], x_prompt.shape[1]
    pos_p = jnp.arange(Tp)
    h0 = jnp.zeros((N_A_LAYERS, Bp, D_MODEL), x_prompt.dtype)
    s0 = jnp.zeros((N_A_LAYERS, Bp, RW_HEADS, RW_HEAD, RW_HEAD), jnp.float32)
    y_prompt, ckv_prompt, kpe_prompt, wkv_prompt, shift_prompt = trunk(
        x_prompt, c_prompt, pos_p, h0, s0, None, None, W)
    pos_s = cache_ckv.shape[1] + jnp.arange(x_sample.shape[1])
    y_sample, ckv_sample, kpe_sample, wkv_sample, shift_sample = trunk(
        x_sample, c_sample, pos_s, state_shift, state_wkv, cache_ckv, cache_kpe, W)
    return (y_prompt, y_sample, ckv_prompt, kpe_prompt, wkv_prompt, shift_prompt,
            ckv_sample, kpe_sample, wkv_sample, shift_sample)


_drawn_inputs = setup_inputs


def setup_inputs(seed=0):
    import zlib

    import numpy as np

    out = dict(_drawn_inputs(seed))
    spreads = {}
    factors = {'cache_kpe': 3.449, 'rw_lnx_g': 7.097, 'rw_lnx_b': 8.0, 'kv_ada_b': 4.144, 'mla_q_g': 8.0}
    for name, (base, spread) in spreads.items():
        noise = np.random.default_rng([zlib.crc32(name.encode()), seed]).standard_normal(out[name].shape)
        drawn = base * np.exp(spread * noise) if base else spread * noise
        out[name] = __import__('jax').numpy.asarray(drawn.astype(out[name].dtype))
    for name, factor in factors.items():
        out[name] = (out[name] * factor).astype(out[name].dtype)
    return out
```

```python
from contextlib import ExitStack

import numpy as np
import concourse.bass as bass
from concourse import mybir

F32 = mybir.dt.float32
F32R = mybir.dt.float32r
ALU = mybir.AluOpType
ACT = mybir.ActivationFunctionType
AX = mybir.AxisListType

P = 128
D = 2048
KB = D // P
TP, TS = 256, 32
T = TP + TS
C = 64
NCH = TP // C + 1
TT = NCH * C
PAST = 128
KEYS = TP + PAST + TS
SK = PAST + TS
HEADS = 32
KV = 512
NOPE, ROPE, VD = 128, 64, 128
SCALE = float((NOPE + ROPE) ** -0.5)
EPS = 1e-6
GN_EPS = 64e-5
HS = 1024
RAW, SPL = 8, 4
LEVELS = 6
DEC = float(np.exp(-0.5))
HOIST = 3

ADAB = 0
MOD_BLOCKS = 2 * 6 * KB + 2 * KB
G_MIX0, G_MLP0, G_MIX1, G_MLP1, G_KV, G_FIN = [MOD_BLOCKS + KB * i for i in range(6)]
MU = G_FIN + KB
SHIFT = MU + 6 * KB
LATG = SHIFT + KB
QG = LATG + 4
NVEC = QG + 4
IDENT, ONES_D, ONES_Q, BD1, BD64 = [P * i for i in range(5)]
MASK_S = 5 * P
MASK_I = MASK_S + C
MASK_L = MASK_I + C
EYE2 = MASK_L + LEVELS * C
CARRY = EYE2 + C
SEL = CARRY + TT
NCONST = SEL + 2
LW_W, LW_A, LW_G, LW_P = 0, P, 2 * P, 4 * P
PW0, PA0, PKK, PKA, PRK, PLG, PLB = range(LW_P, LW_P + 7)
NLW = 4 * P + 8
Z, SSQ, GRAM, TOK = range(1, 5)
Y, MEAN, VAR, GATE = range(1, 5)
SCAN_CHAIN = 2 * (2 + 13 + 4)


class Stage:

    def __init__(self, name, groups, per, mixed=False, epi=None, src=None, gate=None):
        self.name, self.groups, self.per = name, groups, per
        self.mixed, self.epi, self.src, self.gate = mixed, epi, src, gate
        self.wide = 2 if self.mixed else 1


def plan():
    st = [Stage("ada0", 8, 8)]
    for n in ("r", "k", "v"):
        st.append(Stage(n, 4, 16, mixed=True, epi="copy", src="A"))
    st.append(Stage("o", 4, 16, mixed=True, epi="resid", src="A", gate=2))
    for c in range(4):
        st.append(Stage(f"m1_0_{c}", 4, 16, mixed=True, epi="relu2", src="A"))
        st.append(Stage(f"m2_0_{c}", 4, 16, mixed=True, epi="resid", src="B", gate=5))
    st.append(Stage("kvd", 1, 10, src="A"))
    st.append(Stage("wdq", 1, 8, src="A"))
    st.append(Stage("att0", 4, 8))
    st.append(Stage("wo0", 4, 8, epi="resid", src="A", gate=8))
    st.append(Stage("att1", 4, 8))
    st.append(Stage("wo1", 4, 8, epi="resid", src="A", gate=8))
    for c in range(4):
        st.append(Stage(f"m1_1_{c}", 4, 8, epi="relu2", src="A"))
        st.append(Stage(f"m2_1_{c}", 4, 8, epi="resid", src="B", gate=11))
    n = ada = gd = hidden = 0
    free = [0] * 4
    makers = ["r", "k", "v", "o", "m1_0_0", "kvd", "wdq", "wo0", "wo1", "m1_1_0"]
    a0 = 0
    for s in st:
        s.n0, s.ada0, s.gd0, s.free0, s.hid0 = n, ada, gd, list(free), hidden
        n += s.groups * s.per
        if s.mixed or s.name == "ada0":
            ada += s.groups
        if s.name in makers:
            a0 = KB * makers.index(s.name)
        s.a0 = a0
        if s.name == "kvd":
            gd, free = gd + 5, [f + 1 for f in free]
        elif s.name == "wdq":
            gd, free = gd + 4, [f + 1 for f in free]
        elif s.epi:
            gd, free = gd + 3 * 4, [f + 4 for f in free]
        if s.epi == "relu2":
            hidden += KB
        if s.src == "B":
            s.hid0 -= KB
    return st, n, free


ST, NSLOTS, FREE_END = plan()
BY = {s.name: s for s in ST}
NORMS = [(KB, 0), (KB, BY["m1_0_0"].free0[3]), (KB, BY["kvd"].free0[3]), (4, 0), (KB, 0), (4, 0),
         (KB, BY["m1_1_0"].free0[3]), (KB, FREE_END[3])]
N_MIX0, N_MLP0, N_KV, N_LAT, N_MIX1, N_Q, N_MLP1, N_FIN = range(8)
SQ0 = [sum(n for n, _ in NORMS[:i]) for i in range(9)]
MODULATED = {N_MIX0: 0, N_MLP0: 1, N_KV: 2, N_MIX1: 3, N_MLP1: 4}
NORM_MOD = {N_MIX0: (0, KB, G_MIX0, 8, None), N_MLP0: (3 * KB, 4 * KB, G_MLP0, 20, "m1_0_0"),
            N_KV: (12 * KB, 13 * KB, G_KV, 56, "kvd"), N_MIX1: (6 * KB, 7 * KB, G_MIX1, 56, "wdq"),
            N_MLP1: (9 * KB, 10 * KB, G_MLP1, 56, "m1_1_0")}


def addr_plan():
    sizes = [("RAW", RAW * HS * 4), ("HI", SPL * HS * 4), ("LO", SPL * HS * 4), ("AH", KB * T * 4),
             ("AL", KB * T * 4), ("R", KB * TT * 4), ("K", KB * TT * 4), ("V", KB * TT * 4),
             ("H", KB * (T + 2) * 4 + 32), ("WORK", 7 * T * 4), ("SPARE", 6144), ("CONST", NCONST * 4 + 24),
             ("VEC", NVEC * 4 + 32), ("MOD", MOD_BLOCKS * 8), ("SMALL", 1024), ("MIDS", 4 * T * 4)]
    at, out = 16512, {}
    for n, s in sizes:
        at = (at + 31) // 32 * 32
        out[n] = at
        at += s
    out["END"] = at
    assert at <= 229344, at
    return out


class Count:

    def __init__(self, eng, sem):
        self.eng, self.sem, self.n, self.off = eng, sem, 0, 0

    def inc(self, ins):
        ins.then_inc(self.sem, 1)
        self.n += 1
        return ins

    def wait(self):
        self.eng.wait_ge(self.sem, self.off + self.n)

    def start(self, it, per):
        self.n0, self.per, self.off = self.n, per, it * per

    def end(self, rounds):
        assert self.n - self.n0 == self.per, (self.n - self.n0, self.per)
        self.n, self.off = self.n0 + self.per * rounds, 0


def trunk(nc, d):
    es = ExitStack()
    at = addr_plan()

    def sb(name, shape, region, off=0, dt=F32):
        return nc.alloc_sbuf_tensor_at("sb_" + name, shape, dt, offset=at[region] + off)

    def sem(name):
        return es.enter_context(nc.semaphore("sem_" + name))

    with es:
        PS = es.enter_context(nc.psum_tensor("ps", [P, 8, 512], F32))
        raw = sb("raw", [P, RAW, HS], "RAW")
        whi = sb("whi", [P, SPL, HS], "HI", dt=F32R)
        wlo = sb("wlo", [P, SPL, HS], "LO", dt=F32R)
        ah = sb("ah", [P, KB, T], "AH", dt=F32R)
        al = sb("al", [P, KB, T], "AL", dt=F32R)
        x = sb("x", [P, KB, T], "R")
        r = sb("r", [P, KB, TT], "R")
        k = sb("k", [P, KB, TT], "K")
        v = sb("v", [P, KB, TT], "V")
        bh = sb("bh", [P, KB, T], "K", dt=F32R)
        bl = sb("bl", [P, KB, T], "K", KB * T * 4, dt=F32R)
        hb = sb("hb", [P, KB, T + 2], "H")
        work = sb("work", [P, 7, T], "WORK")
        arow = sb("arow", [4, 512], "SPARE")
        con = sb("con", [P, NCONST], "CONST")
        vec = sb("vec", [P, NVEC], "VEC")
        mod = sb("mod", [P, MOD_BLOCKS, 2], "MOD")
        gs = sb("gs", [P, KB, 2], "SMALL")
        cs = sb("cs", [P, KB, 2], "SMALL", 128)
        csg = sb("csg", [P, KB, 2], "SMALL", 256)
        c4 = sb("c4", [P, KB, 4], "SMALL", 384, dt=F32R)
        eps = sb("eps", [P, 2], "SMALL", 640)
        last = sb("last", [P, 2, KB], "SMALL", 672)
        mxs = sb("mxs", [P, 9], "SMALL", 800)
        sms = sb("sms", [P, 9], "SMALL", 864)
        rsm = sb("rsm", [P, 9], "SMALL", 928)
        mids = sb("mids", [P, 4, T], "MIDS")
        l1w = sb("l1w", [P, KB, 96], "K")
        l1a = sb("l1a", [P, KB, 96], "K", KB * 96 * 4)
        l1g = sb("l1g", [P, KB, 256], "K", 2 * KB * 96 * 4)

        lanes = []
        for u in range(2):
            region, off = ("HI", "H")[u], 0
            t = {}
            for name, shape in ([("lw", [P, NLW])] + [(f"t{i}", [P, TT]) for i in range(6)]
                                + [("e", [P, NCH, C + 1])] + [(n, [P, NCH, P]) for n in ("bk", "nbd", "qbd", "xbd")]
                                + [(n, [P, 2, NCH, C]) for n in ("wl", "sv", "uv", "gr")]
                                + [("w", [P, C]), ("sd", [P, C]), ("st", [P, 2, C])]):
                t[name] = sb(f"{name}{u}", shape, region, off)
                size = 4
                for z in shape[1:]:
                    size *= z
                off += (size + 31) // 32 * 32
            limit = (at["AH"] - at["HI"], at["CONST"] - at["H"])[u]
            assert off <= limit, (off, limit)
            lanes.append(t)

        def att(name, shape, dt=F32, state={"off": 0}):
            out = nc.alloc_sbuf_tensor_at("sb_" + name, shape, dt, offset=at["K"] + state["off"])
            size = 4
            for z in shape[1:]:
                size *= z
            state["off"] += (size + 31) // 32 * 32
            assert at["K"] + state["off"] <= at["WORK"], name
            return out

        kyh = att("kyh", [P, 4, KEYS], F32R)
        kyl = att("kyl", [P, 4, KEYS], F32R)
        kpe = att("kpe", [66, KEYS])
        cqh = att("cqh", [P, 4, T], F32R)
        cql = att("cql", [P, 4, T], F32R)
        kt = att("kt", [P, 4, KEYS])
        vt = att("vt", [P, 4, 512])
        qn = att("qn", [P, 4, T])
        qp = att("qp", [66, 4, T])
        pr = att("pr", [P, 4, 384])
        pt = att("pt", [P, 2, 384])
        trig = sb("trig", [P, T], "MIDS")
        prs = sb("prs", [P, SK], "MIDS", T * 4)
        pts = sb("pts", [P, 2, P], "MIDS", T * 4 + SK * 4)
        lat = kt
        cache = vt

        ident = con[:, IDENT:IDENT + P]
        mask_s = con[:, MASK_S:MASK_S + C]
        mask_i = con[:, MASK_I:MASK_I + C]
        eye2 = con[:, EYE2:EYE2 + C]

        landed = [sem(f"landed{i}") for i in range(RAW)]
        hi_ready, lo_ready, slot_used = sem("hi_ready"), sem("lo_ready"), sem("slot_used")
        gemm_done = sem("gemm_done")
        bank_free = [sem(f"bank_free{i}") for i in range(4)]
        arow_ready, ada_fin, mod_ready = sem("arow_ready"), sem("ada_fin"), sem("mod_ready")
        consts_in, vec_in, c_in, x_in, lora1_in, y_out = (
            sem(n) for n in ("consts_in", "vec_in", "c_in", "x_in", "lora1_in", "y_out"))
        c_sig, c4_ready, eps_ready = sem("c_sig"), sem("c4_ready"), sem("eps_ready")
        a_ready, b_ready, sqhi_done = sem("a_ready"), sem("b_ready"), sem("sqhi_done")
        dve_chain, hid_sq = sem("dve_chain"), sem("hid_sq")
        sq_ready, sq_used, root_done, scaled, mod_done, nhi_done, gs_done = (
            sem(n) for n in ("sq_ready", "sq_used", "root_done", "scaled", "mod_done", "nhi_done", "gs_done"))
        mix_ready, mix_used, mixhi_done, mids_done = (
            sem(n) for n in ("mix_ready", "mix_used", "mixhi_done", "mids_done"))
        last_ready, last_out = sem("last_ready"), sem("last_out")
        lane_sems = ("lane_in vc pre_mm sg sq cum ex nrm prep masked tokc bv q qs qb p1 p2 xu xtu xtb xf w wc u uca ucd "
                     "sp sd sn yc yd ys vs post_mm yg oh free sto").split()
        L = [{n: sem(f"{n}_{u}") for n in lane_sems} for u in range(2)]
        att_sems = ("cache_in trig_in rows_in keys_hi keys_ready cachehi pe_done lat_scaled cqhi cq_ready "
                    "kt_acc kt_done v_acc v_done qn_acc qn_done qr_acc qr_done s_acc nmx ex nrmd "
                    "pt_acc pt_done pts_acc pts_done o_acc ohi kpe_out ckv_out").split()
        S = {n: sem("at_" + n) for n in att_sems}
        y_ready, x_back = sem("y_ready"), sem("x_back")

        block = es.enter_context(nc.Block())

        def rounds(eng, first, end, body):
            if end - first == 1:
                body(first)
            elif end > first:
                with eng.Fori(first, end) as it:
                    body(it)

        def flat(ap):
            return ap.rearrange("p a t -> p (a t)")

        def bank_wait(eng, s, it, m):
            if m < 3:
                eng.wait_ge(gemm_done, 3 * it + (s.gd0 + m + 1))
            else:
                eng.wait_ge(slot_used, s.per * it + (s.n0 + s.per))

        def reader_done(eng, s, p):
            eng.wait_ge(slot_used, s.n0 + (s.groups - 1) * s.per + s.wide * (p + 1))

        def walk(eng, s, nxt, split, produce, epi, row, mods):
            def group(it, after, make=None):
                if make is None:
                    for j in range(HOIST, s.per):
                        split(s, j, it)
                else:
                    for p in range(KB // 2):
                        make(p)
                        for j in range(s.wide * p + HOIST, min(s.wide * (p + 1) + HOIST, s.per)):
                            split(s, j, it)
                if s.mixed:
                    row(s, it)
                if after is not None:
                    for j in range(HOIST):
                        split(after, (s.per if after is s else 0) + j, it if after is s else 0)
                epi(s, it)
                if s.mixed:
                    mods(s.ada0 + it)

            if produce is not None:
                group(0, s, produce)
            rounds(eng, 0 if produce is None else 1, 3, lambda it: group(it, s))
            group(3, BY[nxt] if nxt else None)

        def no(*_):
            pass

        @block.sync
        def _(sp):
            sp.dma_start(csg[:], d["cT"]).then_inc(c_in, 16)
            sp.dma_start(con[:], d["con"]).then_inc(consts_in, 16)
            sp.dma_start(vec[:], d["vec"]).then_inc(vec_in, 16)
            for n in range(RAW):
                sp.dma_start(raw[:, n, :], d["stream"][n]).then_inc(landed[n], 16)
            sp.dma_start(x[:], d["xT"]).then_inc(x_in, 16)
            sp.dma_start(l1w[:], d["l1w"]).then_inc(lora1_in, 16)
            sp.dma_start(l1a[:], d["l1a"]).then_inc(lora1_in, 16)
            sp.dma_start(l1g[:], d["l1g"]).then_inc(lora1_in, 16)
            with sp.Fori(1, NSLOTS // RAW) as i:
                for q in range(RAW):
                    sp.wait_ge(lo_ready, i * RAW + (q + 1 - RAW))
                    sp.dma_start(raw[:, q, :], d["stream"][bass.ds(i * RAW + q, 1)].rearrange("a p c -> (a p) c")
                                 ).then_inc(landed[q], 16)
            for n in range(NSLOTS // RAW * RAW, NSLOTS):
                sp.wait_ge(lo_ready, n + 1 - RAW)
                sp.dma_start(raw[:, n % RAW, :], d["stream"][n]).then_inc(landed[n % RAW], 16)
            sp.wait_ge(y_ready, KB)
            sp.dma_start(d["yT"], x[:]).then_inc(y_out, 16)
            sp.wait_ge(y_out, 16)

        @block.gpsimd
        def _(pool):
            pool.wait_ge(last_ready, 1)
            pool.dma_start(d["shiftT"], last[:]).then_inc(last_out, 16)

            def body(it):
                for u in range(2):
                    t, m = lanes[u], L[u]
                    pool.wait_ge(m["free"], it + 1)
                    pool.dma_start(t["lw"][:], d["lw"][bass.ds(2 * it + u, 1)].rearrange("a p c -> (a p) c")
                                   ).then_inc(m["lane_in"], 16)
                    for z in range(2):
                        p = slice(64 * z, 64 * z + 64)
                        pool.dma_start(t["sv"][p, z, NCH - 1, :],
                                       d["s0"][bass.ds(2 * it + u, 1), p].rearrange("a p c -> (a p) c")
                                       ).then_inc(m["lane_in"], 16)
                for u in range(2):
                    t, m = lanes[u], L[u]
                    pool.wait_ge(m["sn"], 2 * NCH * it + 2 * NCH)
                    pool.dma_start(d["wkvT"][bass.ds(2 * it + u, 1)].rearrange("a p s c -> (a p) s c"), t["st"][:]
                                   ).then_inc(m["sto"], 16)
                    pool.wait_ge(m["sto"], 16 * it + 16)
            rounds(pool, 0, KB // 2, body)
            for u in range(2):
                pool.wait_ge(L[u]["free"], KB // 2 + 1)
            pool.dma_start(x[:], d["xT"]).then_inc(x_back, 16)
            pool.dma_start(trig[:], d["trig"]).then_inc(S["trig_in"], 16)
            pool.wait_ge(slot_used, BY["kvd"].n0)
            pool.dma_start(cache[:, :, 0:PAST], d["cckv"]).then_inc(S["cache_in"], 16)
            pool.dma_start(kpe[0:64, TP:TP + PAST], d["ckpe"]).then_inc(S["rows_in"], 16)
            pool.dma_start(kpe[64:66, :], d["krow"]).then_inc(S["rows_in"], 16)
            for h in range(4):
                pool.dma_start(qp[64:66, h, :], d["qrow"]).then_inc(S["rows_in"], 16)
            pool.wait_ge(S["lat_scaled"], 4)
            pool.dma_start(d["ckvT"], lat[:, :, 0:T]).then_inc(S["ckv_out"], 16)
            pool.wait_ge(S["pe_done"], 2)
            pool.dma_start(d["kpeT"][:, 0:TP], kpe[0:64, 0:TP]).then_inc(S["kpe_out"], 16)
            pool.dma_start(d["kpeT"][:, TP:T], kpe[0:64, TP + PAST:KEYS]).then_inc(S["kpe_out"], 16)
            pool.wait_ge(last_out, 16)
            pool.wait_ge(S["ckv_out"], 16)
            pool.wait_ge(S["kpe_out"], 32)

        @block.scalar
        def _(act):
            def split(s, j, it=0):
                n, step = s.n0 + j, it * s.per
                act.wait_ge(landed[n % RAW], step * 2 + 16 * (n // RAW + 1))
                if n >= SPL or not isinstance(it, int):
                    act.wait_ge(slot_used, step + (n - SPL + 1))
                nc.scalar.activation(whi[:, n % SPL, :], raw[:, n % RAW, :], ACT.Copy).then_inc(hi_ready, 1)

            def epi(s, it):
                if s.epi == "copy":
                    dst = {"r": r, "k": k, "v": v}[s.name]
                    for m in range(4):
                        bank_wait(act, s, it, m)
                        nc.scalar.activation(flat(dst[:, bass.ds(4 * it + m, 1), 0:T]),
                                             PS[:, m, 0:T], ACT.Copy).then_inc(bank_free[m], 1)
                elif s.epi == "relu2":
                    for m in range(4):
                        i = s.hid0 + m
                        bank_wait(act, s, it, m)
                        if i >= 2:
                            act.wait_ge(b_ready, 4 * it + (i - 1))
                        nc.scalar.activation(work[:, m % 2, :], PS[:, m, 0:T], ACT.Relu).then_inc(bank_free[m], 1)
                        act.wait_ge(bank_free[m], it + (s.free0[m] + 1))
                        nc.scalar.activation(flat(bh[:, bass.ds(4 * it + m, 1), :]),
                                             work[:, m % 2, :], ACT.Square).then_inc(sqhi_done, 1)

            def gemm(name, nxt, produce=None):
                walk(act, BY[name], nxt, split, produce, epi, no, no)

            def norm_root(i, src):
                nb, need = NORMS[i]
                if i == N_MIX0:
                    act.wait_ge(x_in, 16)
                elif need:
                    act.wait_ge(bank_free[3], need)
                for b in range(nb):
                    q = SQ0[i] + b
                    if q >= 2:
                        act.wait_ge(sq_used, q - 1)
                    if i == N_LAT:
                        act.wait_ge(bank_free[b], BY["kvd"].free0[b] + 1)
                    if i == N_Q:
                        act.wait_ge(bank_free[b], BY["wdq"].free0[b] + 1)
                    nc.scalar.activation(work[:, b % 2, :], src[:, b, 0:T], ACT.Square).then_inc(sq_ready, 1)
                act.wait_ge(sq_used, SQ0[i + 1])
                nc.scalar.activation(work[:, 6, :], PS[:, 6, 0:T], ACT.Sqrt, bias=eps[:, 0:1]).then_inc(root_done, 1)

            def modulate(i, b, to_h):
                q = KB * MODULATED[i] + b
                sh = NORM_MOD[i][0]
                if b == 0:
                    act.wait_ge(gs_done, MODULATED[i] + 1)
                act.wait_ge(scaled, q + 1)
                if to_h:
                    dst = (hb[:, b, 1:1 + TP], hb[:, b, TP + 2:T + 2])
                else:
                    if b >= 2:
                        act.wait_ge(a_ready, BY[NORM_MOD[i][4]].a0 + b - 1)
                    dst = (work[:, 4 + b % 2, 0:TP], work[:, 4 + b % 2, TP:T])
                for z, cols in ((0, slice(0, TP)), (1, slice(TP, T))):
                    nc.scalar.activation(dst[z], work[:, 2 + b % 2, cols], ACT.Identity,
                                         bias=mod[:, sh + b, z:z + 1], scale=gs[:, b, z:z + 1]).then_inc(mod_done, 1)
                if not to_h:
                    act.wait_ge(mod_done, 2 * (q + 1))
                    nc.scalar.activation(ah[:, b, :], work[:, 4 + b % 2, :], ACT.Copy).then_inc(nhi_done, 1)

            def norm_pair(i):
                return lambda p: [modulate(i, b, False) for b in (2 * p, 2 * p + 1)]

            def mix_pair(i, before):
                def pair(p):
                    if before:
                        reader_done(act, BY[before], p)
                    for b in (2 * p, 2 * p + 1):
                        act.wait_ge(mix_ready, KB * (3 + i) + b + 1)
                        nc.scalar.activation(ah[:, b, :], work[:, 2 + b % 2, :], ACT.Copy).then_inc(mixhi_done, 1)
                return pair

            act.wait_ge(c_in, 16)
            nc.scalar.activation(cs[:], csg[:], ACT.Sigmoid).then_inc(c_sig, 1)
            act.wait_ge(eps_ready, 2)
            s = BY["ada0"]
            for j in range(8 + HOIST):
                split(s, j)

            def body(it):
                for j in range(HOIST, 8):
                    split(s, j, it)
                for j in range(HOIST):
                    split(s, 8 + j, it)
            rounds(act, 1, 7, body)
            for j in range(HOIST, 8):
                split(s, 56 + j)
            for j in range(HOIST):
                split(BY["r"], j)
            norm_root(N_MIX0, x)
            for b in range(KB):
                modulate(N_MIX0, b, True)

            for i, f in enumerate((ACT.Tanh, ACT.Copy, ACT.Sigmoid)):
                act.wait_ge(mix_used, KB * (i + 1))
                for z in range(2 if i == 2 else 1):
                    m = 96 if i < 2 else P
                    nc.scalar.activation(mids[0:m, i + z, :], PS[0:m, i + z, 0:T], f).then_inc(mids_done, 1)

            gemm("r", "k", mix_pair(0, None))
            gemm("k", "v", mix_pair(1, "r"))
            gemm("v", None, mix_pair(2, "k"))

            def body(it):
                for u in range(2):
                    t, m = lanes[u], L[u]
                    act.wait_ge(m["pre_mm"], 4 * it + Z)
                    nc.scalar.activation(t["t0"][:, 0:T], PS[:, 4 * u, 0:T], ACT.Sigmoid,
                                         bias=t["lw"][:, PW0:PW0 + 1]).then_inc(m["sg"], 1)
                    nc.scalar.activation(t["t1"][:, 0:T], PS[:, 4 * u + 1, 0:T], ACT.Sigmoid,
                                         bias=t["lw"][:, PA0:PA0 + 1]).then_inc(m["sg"], 1)
                    nc.scalar.activation(t["t2"][:], flat(k[:, bass.ds(2 * it + u, 1), :]), ACT.Square,
                                         scale=t["lw"][:, PKK:PKK + 1]).then_inc(m["sq"], 1)
                for u in range(2):
                    t, m = lanes[u], L[u]
                    act.wait_ge(m["cum"], it + 1)
                    cum = t["t3"][:].rearrange("p (c t) -> p c t", c=NCH)
                    nc.scalar.activation(t["e"][:, :, 1:C + 1], cum, ACT.Exp, scale=-DEC).then_inc(m["ex"], 1)
                    nc.scalar.activation(t["t4"][:], t["t3"][:], ACT.Exp, scale=DEC).then_inc(m["ex"], 1)
                for u in range(2):
                    t, m = lanes[u], L[u]
                    act.wait_ge(m["pre_mm"], 4 * it + SSQ)
                    nc.scalar.activation(t["t2"][:], PS[:, 4 * u + 2, 0:TT], ACT.Sqrt).then_inc(m["nrm"], 1)
                for u in range(2):
                    t, m = lanes[u], L[u]
                    act.wait_ge(m["prep"], it + 1)
                    nc.scalar.activation(t["t5"][:], flat(v[:, bass.ds(2 * it + u, 1), :]), ACT.Copy).then_inc(m["vc"], 1)
                for u in range(2):
                    t, m = lanes[u], L[u]
                    act.wait_ge(m["pre_mm"], 4 * it + TOK)
                    nc.scalar.activation(t["bk"][:, 0:4, :], PS[:, 4 * u, :].rearrange("p (c t) -> p c t", c=4),
                                         ACT.Copy).then_inc(m["tokc"], 1)
                    nc.scalar.activation(t["bk"][:, 4, :], PS[:, 4 * u + 1, 0:P], ACT.Copy).then_inc(m["tokc"], 1)
                    vps = PS[:, 4 * u + 2, 0:TT].rearrange("p (c t) -> p c t", c=NCH)
                    for n in ("sv", "uv"):
                        nc.scalar.activation(t[n][64:128, 0, :, :], vps[64:128], ACT.Copy).then_inc(m["tokc"], 1)
                        nc.scalar.activation(t[n][0:64, 1, :, :], vps[0:64], ACT.Copy).then_inc(m["tokc"], 1)
                for l in range(LEVELS):
                    for u in range(2):
                        t, m = lanes[u], L[u]
                        act.wait_ge(m["qs"], LEVELS * it + l + 1)
                        q = t["t4"][:].rearrange("p (c t) -> p c t", c=NCH)
                        nc.scalar.activation(t["qbd"][0:64, :, 0:64], q[0:64], ACT.Copy).then_inc(m["qb"], 1)
                        nc.scalar.activation(t["qbd"][64:128, :, 64:128], q[64:128], ACT.Copy).then_inc(m["qb"], 1)
                    if l < LEVELS - 1:
                        for u in range(2):
                            t, m = lanes[u], L[u]
                            act.wait_ge(m["xtu"], (LEVELS - 1) * it + l + 1)
                            q = t["t5"][:].rearrange("p (c t) -> p c t", c=NCH)
                            nc.scalar.activation(t["xbd"][0:64, :, 0:64], q[0:64], ACT.Copy).then_inc(m["xtb"], 1)
                            nc.scalar.activation(t["xbd"][64:128, :, 64:128], q[64:128], ACT.Copy).then_inc(m["xtb"], 1)
                for c in range(NCH):
                    for u in range(2):
                        t, m = lanes[u], L[u]
                        if c == NCH - 1:
                            act.wait_ge(m["lane_in"], 48 * it + 48)
                        if c:
                            act.wait_ge(m["sn"], 2 * NCH * it + 2 * c)
                        for z in range(2):
                            p = slice(64 * z, 64 * z + 64)
                            nc.scalar.activation(t["sd"][p, :], t["sv"][p, z, c, :], ACT.Copy,
                                                 scale=t["e"][p, c, C:C + 1]).then_inc(m["sd"], 1)
                    for u in range(2):
                        t, m = lanes[u], L[u]
                        act.wait_ge(m["u"], NCH * it + c + 1)
                        nc.scalar.activation(t["uv"][0:64, 0, c, :], PS[0:64, 4 * u + 1, 0:C], ACT.Copy).then_inc(m["uca"], 1)
                for u in range(2):
                    t, m = lanes[u], L[u]
                    act.wait_ge(m["post_mm"], 4 * it + Y)
                    nc.scalar.activation(t["t2"][0:64, :], PS[0:64, 4 * u, 0:TT], ACT.Copy).then_inc(m["yc"], 1)
                    nc.scalar.activation(t["t2"][64:128, :], PS[64:128, 4 * u + 1, 0:TT], ACT.Copy).then_inc(m["yc"], 1)
                for u in range(2):
                    t, m = lanes[u], L[u]
                    act.wait_ge(m["yd"], it + 1)
                    nc.scalar.activation(t["t3"][:], t["t2"][:], ACT.Square).then_inc(m["ys"], 1)
                for u in range(2):
                    t, m = lanes[u], L[u]
                    act.wait_ge(m["post_mm"], 4 * it + VAR)
                    nc.scalar.activation(t["t3"][:], PS[:, 4 * u + 3, 0:TT], ACT.Sqrt, bias=eps[:, 1:2]).then_inc(m["vs"], 1)
                for u in range(2):
                    t, m = lanes[u], L[u]
                    act.wait_ge(m["yg"], it + 1)
                    nc.scalar.activation(flat(ah[:, bass.ds(2 * it + u, 1), :]), t["t2"][:, 0:T], ACT.Copy).then_inc(m["oh"], 1)
            rounds(act, 0, KB // 2, body)

            for u in range(2):
                act.wait_ge(L[u]["free"], KB // 2 + 1)
                act.wait_ge(L[u]["sto"], 16 * (KB // 2))
            for j in range(HOIST):
                split(BY["o"], j)
            gemm("o", "m1_0_0")
            norm_root(N_MLP0, x)
            for c in range(4):
                gemm(f"m1_0_{c}", f"m2_0_{c}", norm_pair(N_MLP0) if c == 0 else None)
                gemm(f"m2_0_{c}", f"m1_0_{c + 1}" if c < 3 else "kvd")

            norm_root(N_KV, x)
            s = BY["kvd"]
            for p in range(KB // 2):
                norm_pair(N_KV)(p)
                if p + HOIST < s.per:
                    split(s, p + HOIST)
            act.wait_ge(S["cache_in"], 16)
            nc.scalar.activation(kyh[:, :, TP:TP + PAST], cache[:, :, 0:PAST], ACT.Copy).then_inc(S["cachehi"], 1)
            for m in range(4):
                act.wait_ge(gemm_done, s.gd0 + m + 1)
                nc.scalar.activation(lat[:, m, 0:T], PS[:, m, 0:T], ACT.Copy).then_inc(bank_free[m], 1)
            for j in range(HOIST):
                split(BY["wdq"], j)
            norm_root(N_LAT, lat)
            for m in range(4):
                act.wait_ge(S["lat_scaled"], m + 1)
                nc.scalar.activation(kyh[:, m, 0:TP], lat[:, m, 0:TP], ACT.Copy).then_inc(S["keys_hi"], 1)
                nc.scalar.activation(kyh[:, m, TP + PAST:KEYS], lat[:, m, TP:T], ACT.Copy).then_inc(S["keys_hi"], 1)
            norm_root(N_MIX1, x)
            act.wait_ge(slot_used, BY["wdq"].n0)
            s = BY["wdq"]
            for p in range(KB // 2):
                norm_pair(N_MIX1)(p)
                if p + HOIST < s.per:
                    split(s, p + HOIST)
            for j in range(HOIST):
                split(BY["att0"], j)
            for m in range(4):
                act.wait_ge(gemm_done, s.gd0 + m + 1)
                nc.scalar.activation(qn[:, m, :], PS[:, m, 0:T], ACT.Copy).then_inc(bank_free[m], 1)
            norm_root(N_Q, qn)
            for m in range(4):
                act.wait_ge(S["lat_scaled"], 4 + m + 1)
                nc.scalar.activation(cqh[:, m, :], qn[:, m, :], ACT.Copy).then_inc(S["cqhi"], 1)

            act.wait_ge(S["ckv_out"], 16)

            def out_hi(it, h, v4):
                act.wait_ge(S["o_acc"], v4 + h + 1)
                nc.scalar.activation(flat(ah[:, bass.ds(4 * it + h, 1), :]), PS[:, 4 + h, 0:T], ACT.Copy).then_inc(S["ohi"], 1)

            def group(s, g0, it, after):
                v1, v4 = it + (g0 + 1), it * 4 + 4 * g0
                for j in range(HOIST, 6):
                    split(s, j, it)
                for m in range(4):
                    act.wait_ge(S["kt_acc"], v4 + m + 1)
                    nc.scalar.activation(kt[:, m, :], PS[:, m, 0:KEYS], ACT.Copy).then_inc(S["kt_done"], 1)
                for j in range(6, 8):
                    split(s, j, it)
                for m in range(4):
                    act.wait_ge(S["qn_acc"], v4 + m + 1)
                    nc.scalar.activation(qn[:, m, :], PS[:, m, 0:T], ACT.Copy).then_inc(S["qn_done"], 1)
                for j in range(HOIST):
                    split(after or s, j if after else s.per + j, 0 if after else it)
                act.wait_ge(S["nmx"], v1)
                for h in range(4):
                    nc.scalar.activation(pr[:, h, 0:P], PS[:, 4 + h, 0:P], ACT.Exp, scale=SCALE,
                                         bias=mxs[:, h:h + 1], accum_out=sms[:, h:h + 1]).then_inc(S["ex"], 1)
                    nc.scalar.activation(pr[:, h, P:384], PS[:, 4 + h, P:384], ACT.Exp, scale=SCALE,
                                         bias=mxs[:, 4 + h:5 + h], accum_out=sms[:, 4 + h:5 + h]).then_inc(S["ex"], 1)
                nc.scalar.activation(prs[:], PS[:, 0, 0:SK], ACT.Exp, scale=SCALE,
                                     bias=mxs[:, 8:9], accum_out=sms[:, 8:9]).then_inc(S["ex"], 1)
                act.wait_ge(S["pts_acc"], v1)
                nc.scalar.activation(pts[:, 0, :], PS[:, 0, 0:P], ACT.Copy).then_inc(S["pts_done"], 1)
                nc.scalar.activation(pts[0:32, 1, :], PS[0:32, 0, P:2 * P], ACT.Copy).then_inc(S["pts_done"], 1)
                for h in range(4):
                    act.wait_ge(S["pt_acc"], v4 + h + 1)
                    if h >= 2:
                        act.wait_ge(S["o_acc"], v4 + h - 1)
                    nc.scalar.activation(pt[:, h % 2, :], PS[:, 1 + h % 2, 0:384], ACT.Copy).then_inc(S["pt_done"], 1)
                    if h >= 1:
                        out_hi(it, h - 1, v4)
                out_hi(it, 3, v4)

            for half in range(2):
                s = BY[f"att{half}"]
                rounds(act, 0, 3, lambda it: group(s, 4 * half, it, None))
                group(s, 4 * half, 3, BY[f"wo{half}"])
                gemm(f"wo{half}", "m1_1_0" if half else "att1")
            norm_root(N_MLP1, x)
            act.wait_ge(S["kpe_out"], 32)
            for c in range(4):
                gemm(f"m1_1_{c}", f"m2_1_{c}", norm_pair(N_MLP1) if c == 0 else None)
                gemm(f"m2_1_{c}", f"m1_1_{c + 1}" if c < 3 else None)
            norm_root(N_FIN, x)

        @block.vector
        def _(dve):
            ch = Count(dve, dve_chain)

            def split(s, j, it=0):
                n, step = s.n0 + j, it * s.per
                dve.wait_ge(hi_ready, step + (n + 1))
                nc.vector.tensor_tensor(wlo[:, n % SPL, :], raw[:, n % RAW, :], whi[:, n % SPL, :],
                                        ALU.subtract).then_inc(lo_ready, 1)

            def row(s, it):
                g = s.ada0 + it
                used = s.n0 + (s.per - s.wide + 1)
                dve.wait_ge(slot_used, s.per * it + used)
                if s.name != "ada0" or not isinstance(it, int) or it:
                    dve.wait_ge(ada_fin, g)
                nc.vector.tensor_copy(arow[:], PS[0:4, 4, :]).then_inc(arow_ready, 1)

            def mods(g):
                dve.wait_ge(ada_fin, g + 1)
                nc.vector.tensor_tensor(mod[:, bass.ds(4 * g, 4), :],
                                        PS[:, 5, 0:8].rearrange("p (a t) -> p a t", a=4),
                                        vec[:, bass.ds(4 * g + ADAB, 4)].rearrange("p (a t) -> p a t", t=1).to_broadcast([P, 4, 2]),
                                        ALU.add).then_inc(mod_ready, 1)

            def epi(s, it):
                if s.epi == "resid":
                    for m in range(4):
                        bank_wait(dve, s, it, m)
                        for z, cols in ((0, slice(0, TP)), (1, slice(TP, T))):
                            xb = flat(x[:, bass.ds(4 * it + m, 1), cols])
                            ins = nc.vector.scalar_tensor_tensor(
                                out=xb, in0=PS[:, m, cols], scalar=flat(mod[:, bass.ds(4 * it + (KB * s.gate + m), 1), z:z + 1]),
                                in1=xb, op0=ALU.mult, op1=ALU.add)
                        ins.then_inc(bank_free[m], 1)
                elif s.epi == "relu2":
                    for m in range(4):
                        i = s.hid0 + m
                        dve.wait_ge(bank_free[m], it + (s.free0[m] + 1))
                        nc.vector.tensor_tensor(work[:, 2 + m % 2, :], work[:, m % 2, :], work[:, m % 2, :],
                                                ALU.mult).then_inc(hid_sq, 1)
                        dve.wait_ge(hid_sq, 4 * it + (i + 1))
                        dve.wait_ge(sqhi_done, 4 * it + (i + 1))
                        nc.vector.tensor_tensor(flat(bl[:, bass.ds(4 * it + m, 1), :]), work[:, 2 + m % 2, :],
                                                flat(bh[:, bass.ds(4 * it + m, 1), :]), ALU.subtract).then_inc(b_ready, 1)

            def gemm(name, nxt, produce=None):
                walk(dve, BY[name], nxt, split, produce, epi, row, mods)

            def norm_scale(i):
                dve.wait_ge(root_done, i + 1)
                ch.inc(nc.vector.reciprocal(work[:, 6, :], work[:, 6, :]))
                if i in MODULATED:
                    _, sc, gain, need, _ = NORM_MOD[i]
                    dve.wait_ge(mod_ready, need)
                    if MODULATED[i]:
                        dve.wait_ge(mod_done, 2 * KB * MODULATED[i])
                    nc.vector.scalar_tensor_tensor(
                        out=gs[:], in0=mod[:, sc:sc + KB, :], scalar=1.0,
                        in1=vec[:, gain:gain + KB].rearrange("p (a t) -> p a t", t=1).to_broadcast([P, KB, 2]),
                        op0=ALU.add, op1=ALU.mult).then_inc(gs_done, 1)
                ch.wait()

            def scale_block(i, b):
                q = KB * MODULATED[i] + b
                if q >= 2:
                    dve.wait_ge(mod_done, 2 * (q - 1))
                nc.vector.tensor_tensor(work[:, 2 + b % 2, :], x[:, b, :], work[:, 6, :], ALU.mult).then_inc(scaled, 1)

            def norm_pair(i):
                def pair(p):
                    for b in (2 * p, 2 * p + 1):
                        scale_block(i, b)
                    for b in (2 * p, 2 * p + 1):
                        dve.wait_ge(nhi_done, KB * (MODULATED[i] - 1) + b + 1)
                        nc.vector.tensor_tensor(al[:, b, :], work[:, 4 + b % 2, :], ah[:, b, :],
                                                ALU.subtract).then_inc(a_ready, 1)
                return pair

            def mix(col, q, b):
                dd = work[:, 4:6, :].rearrange("p a t -> p (a t)")
                if q:
                    dve.wait_ge(mix_ready, q)
                    ch.wait()
                ch.inc(nc.vector.tensor_tensor(dd[:, 0:T + 1], hb[:, b, 0:T + 1], hb[:, b, 1:T + 2], ALU.subtract))
                ch.wait()
                mu = vec[:, MU + KB * col + b:MU + KB * col + b + 1]
                for z, a, n in ((0, 0, TP), (1, TP + 1, TS)):
                    ins = nc.vector.scalar_tensor_tensor(out=work[:, 2 + b % 2, a - z:a - z + n], in0=dd[:, a:a + n],
                                                         scalar=mu, in1=hb[:, b, a + 1:a + 1 + n],
                                                         op0=ALU.mult, op1=ALU.add)
                    if z:
                        ins.then_inc(mix_ready, 1)
                    else:
                        ch.inc(ins)

            def mix_pair(i, col, before):
                def pair(p):
                    if before:
                        reader_done(dve, BY[before], p)
                    for b in (2 * p, 2 * p + 1):
                        q = KB * i + b
                        if q >= 2:
                            dve.wait_ge(mixhi_done, q - 1)
                        mix(col, KB * (3 + i) + b, b)
                    for b in (2 * p, 2 * p + 1):
                        dve.wait_ge(mixhi_done, KB * i + b + 1)
                        nc.vector.tensor_tensor(al[:, b, :], work[:, 2 + b % 2, :], ah[:, b, :],
                                                ALU.subtract).then_inc(a_ready, 1)
                return pair

            nc.vector.memset(eps[:, 0:1], EPS).then_inc(eps_ready, 1)
            nc.vector.memset(eps[:, 1:2], GN_EPS).then_inc(eps_ready, 1)
            ch.inc(nc.vector.memset(hb[:, :, 0:1], 0.0))
            dve.wait_ge(vec_in, 16)
            dve.wait_ge(consts_in, 16)
            ch.inc(nc.vector.tensor_copy(hb[:, :, TP + 1:TP + 2], vec[:, SHIFT:SHIFT + KB].rearrange("p (a t) -> p a t", t=1)))
            dve.wait_ge(c_sig, 1)
            ch.inc(nc.vector.tensor_tensor(cs[:], cs[:], csg[:], ALU.mult))
            ch.wait()
            ch.inc(nc.vector.tensor_copy(c4[:, :, 0:2], cs[:]))
            ch.wait()
            nc.vector.tensor_tensor(c4[:, :, 2:4], cs[:], c4[:, :, 0:2], ALU.subtract).then_inc(c4_ready, 1)

            s = BY["ada0"]
            for j in range(8 + HOIST):
                split(s, j)
                if j == 7:
                    row(s, 0)
            mods(0)

            def body(it):
                for j in range(HOIST, 8):
                    split(s, j, it)
                row(s, it)
                for j in range(HOIST):
                    split(s, 8 + j, it)
                mods(it)
            rounds(dve, 1, 7, body)
            for j in range(HOIST, 8):
                split(s, 56 + j)
            row(s, 7)
            for j in range(HOIST):
                split(BY["r"], j)
            mods(7)

            norm_scale(N_MIX0)
            for b in range(KB):
                scale_block(N_MIX0, b)
            dve.wait_ge(mod_done, 2 * KB)
            ch.inc(nc.vector.tensor_copy(last[:, 0, :], hb[:, :, TP:TP + 1].rearrange("p a t -> p (a t)")))
            ch.wait()
            nc.vector.tensor_copy(last[:, 1, :], hb[:, :, T + 1:T + 2].rearrange("p a t -> p (a t)")).then_inc(last_ready, 1)
            for i, col in enumerate((1, 4, 5)):
                for b in range(KB):
                    q = KB * i + b
                    if q >= 2:
                        dve.wait_ge(mix_used, q - 1)
                    mix(col, q, b)
            dve.wait_ge(mix_used, 3 * KB)
            gemm("r", "k", mix_pair(0, 0, None))
            gemm("k", "v", mix_pair(1, 2, "r"))
            gemm("v", None, mix_pair(2, 3, "k"))

            for z in (r, k, v):
                ch.inc(nc.vector.memset(z[:, :, T:TT], 0.0))
            dve.wait_ge(slot_used, BY["o"].n0)
            dve.wait_ge(last_out, 16)
            for u in range(2):
                t, m = lanes[u], L[u]
                for n in ("nbd", "qbd", "xbd"):
                    ch.inc(nc.vector.memset(t[n][:], 0.0))
                ch.inc(nc.vector.memset(t["t0"][:, T:TT], 0.0))
                ch.inc(nc.vector.memset(t["t1"][:, T:TT], 0.0))
                ch.inc(nc.vector.memset(t["e"][:, :, 0:1], 1.0))
                ch.inc(nc.vector.memset(t["sv"][0:64, 0, 0, :], 0.0))
                ch.inc(nc.vector.memset(t["sv"][64:128, 1, 0, :], 0.0))
                ch.wait()
                nc.vector.memset(t["w"][:], 0.0).then_inc(m["free"], 1)

            def body(it):
                ch.start(it, SCAN_CHAIN)
                tt, stt = nc.vector.tensor_tensor, nc.vector.scalar_tensor_tensor

                def c3(ap):
                    return ap.rearrange("p (c t) -> p c t", c=NCH)

                def mask(col, p=slice(0, P)):
                    return con[p, col:col + C].rearrange("p (c t) -> p c t", c=1).to_broadcast([p.stop - p.start, NCH, C])

                top, bot = slice(0, 64), slice(64, 128)
                for u in range(2):
                    t, m = lanes[u], L[u]
                    dve.wait_ge(m["free"], it + 1)
                    ch.inc(nc.vector.memset(t["t0"][:, T:TT], 0.0))
                    ch.inc(nc.vector.memset(t["t1"][:, T:TT], 0.0))
                    ch.wait()
                    dve.wait_ge(m["sg"], 2 * it + 2)
                    nc.vector.tensor_tensor_scan(t["t3"][:], con[:, CARRY:CARRY + TT], t["t0"][:], 0.0,
                                                 ALU.mult, ALU.add).then_inc(m["cum"], 1)
                for u in range(2):
                    t, m = lanes[u], L[u]
                    lw = t["lw"]
                    rb, kb = (flat(z[:, bass.ds(2 * it + u, 1), :]) for z in (r, k))
                    eprev, enow = t["e"][:, :, 0:C], t["e"][:, :, 1:C + 1]
                    dve.wait_ge(m["sg"], 2 * it + 2)
                    dve.wait_ge(m["nrm"], it + 1)
                    ch.inc(nc.vector.tensor_scalar(t["t2"][:], t["t2"][:], 1e-12, None, ALU.max))
                    ch.inc(nc.vector.tensor_scalar(t["t5"][:], t["t1"][:], 1.0, lw[:, PKA:PKA + 1], ALU.subtract, ALU.mult))
                    ch.wait()
                    ch.inc(nc.vector.reciprocal(t["t2"][:], t["t2"][:]))
                    ch.wait()
                    ch.inc(stt(out=t["t2"][:], in0=kb, scalar=lw[:, PKK:PKK + 1], in1=t["t2"][:], op0=ALU.mult, op1=ALU.mult))
                    ch.wait()
                    ch.inc(stt(out=kb, in0=t["t5"][:], scalar=1.0, in1=kb, op0=ALU.add, op1=ALU.mult))
                    ch.inc(tt(t["t1"][:], t["t2"][:], t["t1"][:], ALU.mult))
                    dve.wait_ge(m["ex"], 2 * it + 2)
                    for z, p in ((0, top), (1, bot)):
                        ch.inc(stt(out=t["wl"][p, z, :, :], in0=c3(t["t2"][:])[p], scalar=-1.0, in1=eprev[p],
                                   op0=ALU.mult, op1=ALU.mult))
                    ch.wait()
                    ch.inc(stt(out=t["t0"][:], in0=rb, scalar=lw[:, PRK:PRK + 1], in1=kb, op0=ALU.mult, op1=ALU.mult))
                    for z, p in ((0, top), (1, bot)):
                        ch.inc(tt(t["bk"][p, :, C * z:C * z + C], c3(t["t1"][:])[p], c3(t["t4"][:])[p], ALU.mult))
                        ch.inc(tt(t["bk"][p, :, C - C * z:2 * C - C * z], c3(kb)[p], c3(t["t4"][:])[p], ALU.mult))
                    ch.wait()
                    tt(c3(t["t1"][:]), c3(rb), enow, ALU.mult).then_inc(m["prep"], 1)
                for u in range(2):
                    t, m = lanes[u], L[u]
                    b0 = 4 * u
                    dve.wait_ge(m["pre_mm"], 4 * it + GRAM)
                    ga = [PS[:, b0 + 2 * z, 0:TT].rearrange("p (c t) -> p c t", c=NCH) for z in range(2)]
                    gr = [PS[:, b0 + 1 + 2 * z, 0:TT].rearrange("p (c t) -> p c t", c=NCH) for z in range(2)]
                    tt(t["nbd"][top, :, 0:C], ga[0][top], mask(MASK_S, top), ALU.mult).then_inc(m["masked"], 1)
                    tt(t["nbd"][bot, :, C:P], ga[1][bot], mask(MASK_S, bot), ALU.mult).then_inc(m["masked"], 1)
                    tt(t["wl"][bot, 0, :, :], ga[0][bot], mask(MASK_S, bot), ALU.mult).then_inc(m["masked"], 1)
                    tt(t["wl"][top, 1, :, :], ga[1][top], mask(MASK_S, top), ALU.mult).then_inc(m["masked"], 1)
                    for z in range(2):
                        tt(t["gr"][:, z, :, :], gr[z], mask(MASK_I), ALU.mult).then_inc(m["masked"], 1)
                for u in range(2):
                    t, m = lanes[u], L[u]
                    dve.wait_ge(m["pre_mm"], 4 * it + TOK)
                    tt(t["t0"][:], PS[:, 4 * u + 3, 0:TT], flat(v[:, bass.ds(2 * it + u, 1), :]), ALU.mult).then_inc(m["bv"], 1)
                for l in range(LEVELS):
                    for u in range(2):
                        t, m = lanes[u], L[u]
                        dve.wait_ge(m["q"], LEVELS * it + l + 1)
                        tt(c3(t["t4"][:]), c3(PS[:, 4 * u, 0:TT]), mask(MASK_L + C * l), ALU.mult).then_inc(m["qs"], 1)
                    for u in range(2):
                        t, m = lanes[u], L[u]
                        if l == 0:
                            dve.wait_ge(m["qs"], LEVELS * it + 1)
                            tt(c3(t["t3"][:]), c3(t["t4"][:]), mask(EYE2), ALU.add).then_inc(m["xu"], 1)
                        elif l < LEVELS - 1:
                            dve.wait_ge(m["p1"], (LEVELS - 2) * it + l)
                            tt(t["t3"][:], PS[:, 4 * u + 1, 0:TT], t["t3"][:], ALU.add).then_inc(m["xu"], 1)
                        dve.wait_ge(m["p2"], LEVELS * it + l + 1)
                        p2 = c3(PS[:, 4 * u + 2, 0:TT])
                        if l < LEVELS - 1:
                            other = mask(EYE2) if l == 0 else c3(t["t5"][:])
                            tt(c3(t["t5"][:]), p2, other, ALU.add).then_inc(m["xtu"], 1)
                        else:
                            tt(t["xbd"][top, :, 0:C], p2[top], c3(t["t5"][:])[top], ALU.add).then_inc(m["xf"], 1)
                            tt(t["xbd"][bot, :, C:P], p2[bot], c3(t["t5"][:])[bot], ALU.add).then_inc(m["xf"], 1)
                for c in range(NCH):
                    for u in range(2):
                        t, m = lanes[u], L[u]
                        dve.wait_ge(m["w"], NCH * it + c + 1)
                        nc.vector.tensor_copy(t["w"][:], PS[:, 4 * u, 0:C]).then_inc(m["wc"], 1)
                    for u in range(2):
                        t, m = lanes[u], L[u]
                        dve.wait_ge(m["u"], NCH * it + c + 1)
                        nc.vector.tensor_copy(t["uv"][bot, 1, c, :], PS[bot, 4 * u + 1, 0:C]).then_inc(m["ucd"], 1)
                    for u in range(2):
                        t, m = lanes[u], L[u]
                        dve.wait_ge(m["sp"], NCH * it + c + 1)
                        dve.wait_ge(m["sd"], 2 * NCH * it + 2 * c + 2)
                        for z, p in ((0, top), (1, bot)):
                            dst = t["sv"][p, z, c + 1, :] if c < NCH - 2 else t["st"][p, c - (NCH - 2), :]
                            stt(out=dst, in0=PS[p, 4 * u + 2, 0:C], scalar=t["e"][p, c, C:C + 1], in1=t["sd"][p, :],
                                op0=ALU.mult, op1=ALU.add).then_inc(m["sn"], 1)
                for u in range(2):
                    t, m = lanes[u], L[u]
                    dve.wait_ge(m["post_mm"], 4 * it + MEAN)
                    tt(t["t2"][:], t["t2"][:], PS[:, 4 * u + 2, 0:TT], ALU.subtract).then_inc(m["yd"], 1)
                for u in range(2):
                    t, m = lanes[u], L[u]
                    dve.wait_ge(m["vs"], it + 1)
                    ch.inc(nc.vector.reciprocal(t["t3"][:], t["t3"][:]))
                    dve.wait_ge(m["yd"], it + 1)
                    ch.wait()
                    ch.inc(tt(t["t2"][:], t["t2"][:], t["t3"][:], ALU.mult))
                    ch.wait()
                    ch.inc(nc.vector.tensor_scalar(t["t2"][:], t["t2"][:], t["lw"][:, PLG:PLG + 1], t["lw"][:, PLB:PLB + 1],
                                                   ALU.mult, ALU.add))
                    dve.wait_ge(m["bv"], it + 1)
                    ch.wait()
                    ch.inc(tt(t["t2"][:], t["t2"][:], t["t0"][:], ALU.add))
                    dve.wait_ge(m["post_mm"], 4 * it + GATE)
                    ch.wait()
                    tt(t["t2"][:, 0:T], t["t2"][:, 0:T], PS[:, 4 * u, 0:T], ALU.mult).then_inc(m["yg"], 1)
                for u in range(2):
                    t, m = lanes[u], L[u]
                    dve.wait_ge(m["yg"], it + 1)
                    dve.wait_ge(m["oh"], it + 1)
                    tt(flat(al[:, bass.ds(2 * it + u, 1), :]), t["t2"][:, 0:T],
                       flat(ah[:, bass.ds(2 * it + u, 1), :]), ALU.subtract).then_inc(a_ready, 1)
                    dve.wait_ge(m["sto"], 16 * it + 16)
                    dve.wait_ge(a_ready, 2 * it + (BY["o"].a0 + u + 1))
                    nc.vector.memset(t["t3"][:, 0:1], 0.0).then_inc(m["free"], 1)
                ch.end(KB // 2)
            with dve.Fori(0, KB // 2) as it:
                body(it)

            for u in range(2):
                dve.wait_ge(L[u]["free"], KB // 2 + 1)
            for j in range(HOIST):
                split(BY["o"], j)
            dve.wait_ge(x_back, 16)
            gemm("o", "m1_0_0")
            norm_scale(N_MLP0)
            for c in range(4):
                gemm(f"m1_0_{c}", f"m2_0_{c}", norm_pair(N_MLP0) if c == 0 else None)
                gemm(f"m2_0_{c}", f"m1_0_{c + 1}" if c < 3 else "kvd")

            norm_scale(N_KV)
            s = BY["kvd"]
            for p in range(KB // 2):
                norm_pair(N_KV)(p)
                if p + HOIST < s.per:
                    split(s, p + HOIST)
            for j in range(HOIST):
                split(BY["wdq"], j)
            dve.wait_ge(S["cachehi"], 1)
            nc.vector.tensor_tensor(kyl[:, :, TP:TP + PAST], cache[:, :, 0:PAST], kyh[:, :, TP:TP + PAST],
                                    ALU.subtract).then_inc(S["keys_ready"], 1)

            def rope(src, dst_parts, done):
                ch.inc(nc.vector.tensor_tensor(work[0:64, 4, :], src[0:64], trig[0:64, :], ALU.mult))
                ch.inc(nc.vector.tensor_tensor(work[0:64, 5, :], src[64:128], trig[64:128, :], ALU.mult))
                ch.wait()
                for dst, cols in dst_parts:
                    ins = nc.vector.tensor_tensor(dst, work[0:64, 4, cols], work[0:64, 5, cols], ALU.add)
                    ins.then_inc(done, 1)

            dve.wait_ge(S["trig_in"], 16)
            dve.wait_ge(gemm_done, s.gd0 + 5)
            rope(PS[:, 0, 0:T], ((kpe[0:64, 0:TP], slice(0, TP)), (kpe[0:64, TP + PAST:KEYS], slice(TP, T))), S["pe_done"])

            def latent_scale(i, src, gain, first):
                norm_scale(i)
                for m in range(4):
                    nc.vector.scalar_tensor_tensor(out=src[:, m, 0:T], in0=src[:, m, 0:T], scalar=vec[:, gain + m:gain + m + 1],
                                                   in1=work[:, 6, :], op0=ALU.mult, op1=ALU.mult).then_inc(S["lat_scaled"], 1)
                for m in range(4):
                    if first:
                        dve.wait_ge(S["lat_scaled"], m + 1)
                        dve.wait_ge(S["keys_hi"], 2 * m + 2)
                        for a, b in ((slice(0, TP), slice(0, TP)), (slice(TP + PAST, KEYS), slice(TP, T))):
                            nc.vector.tensor_tensor(kyl[:, m, a], src[:, m, b], kyh[:, m, a], ALU.subtract).then_inc(S["keys_ready"], 1)
                    else:
                        dve.wait_ge(S["lat_scaled"], 4 + m + 1)
                        dve.wait_ge(S["cqhi"], m + 1)
                        nc.vector.tensor_tensor(cql[:, m, :], src[:, m, :], cqh[:, m, :], ALU.subtract).then_inc(S["cq_ready"], 1)

            latent_scale(N_LAT, lat, LATG, True)
            norm_scale(N_MIX1)
            dve.wait_ge(slot_used, BY["wdq"].n0)
            s = BY["wdq"]
            for p in range(KB // 2):
                norm_pair(N_MIX1)(p)
                if p + HOIST < s.per:
                    split(s, p + HOIST)
            for j in range(HOIST):
                split(BY["att0"], j)
            latent_scale(N_Q, qn, QG, False)
            dve.wait_ge(S["ckv_out"], 16)
            dve.wait_ge(S["rows_in"], 96)

            def group(s, g0, it, after):
                v1, v4 = it + (g0 + 1), it * 4 + 4 * g0
                for j in range(HOIST, 7):
                    split(s, j, it)
                for m in range(4):
                    n = P if m < 3 else TS
                    dve.wait_ge(S["v_acc"], v4 + m + 1)
                    nc.vector.tensor_copy(vt[0:n, m, :], PS[0:n, m, :]).then_inc(S["v_done"], 1)
                split(s, 7, it)
                for m in range(4):
                    dve.wait_ge(S["qr_acc"], v4 + m + 1)
                    rope(PS[:, m, 0:T], ((qp[0:64, m, :], slice(0, T)),), S["qr_done"])
                    dve.wait_ge(S["qr_done"], v4 + m + 1)
                for j in range(HOIST):
                    split(after or s, j if after else s.per + j, 0 if after else it)
                dve.wait_ge(S["s_acc"], v1)
                ch.inc(nc.vector.tensor_reduce(mxs[:, 0:4], PS[:, 4:8, 0:P], AX.X, ALU.max))
                ch.inc(nc.vector.tensor_reduce(mxs[:, 4:8], PS[:, 4:8, P:384], AX.X, ALU.max))
                ch.inc(nc.vector.tensor_reduce(mxs[:, 8:9], PS[:, 0, 0:SK], AX.X, ALU.max))
                ch.wait()
                nc.vector.tensor_scalar(mxs[:], mxs[:], -SCALE, None, ALU.mult).then_inc(S["nmx"], 1)
                dve.wait_ge(S["ex"], 9 * v1)
                ch.inc(nc.vector.reciprocal(rsm[:], sms[:]))
                ch.wait()

                def bc(a, n, w):
                    return rsm[:, a:a + n].rearrange("p (a t) -> p a t", t=1).to_broadcast([P, n, w])

                nc.vector.tensor_scalar(prs[:], prs[:], rsm[:, 8:9], None, ALU.mult).then_inc(S["nrmd"], 1)
                nc.vector.tensor_tensor(pr[:, :, 0:P], pr[:, :, 0:P], bc(0, 4, P), ALU.mult).then_inc(S["nrmd"], 1)
                nc.vector.tensor_tensor(pr[:, :, P:384], pr[:, :, P:384], bc(4, 4, 2 * P), ALU.mult).then_inc(S["nrmd"], 1)
                for h in range(4):
                    dve.wait_ge(S["ohi"], v4 + h + 1)
                    nc.vector.tensor_tensor(flat(al[:, bass.ds(4 * it + h, 1), :]), PS[:, 4 + h, 0:T],
                                            flat(ah[:, bass.ds(4 * it + h, 1), :]), ALU.subtract).then_inc(a_ready, 1)

            per = 4 * 2 + 3 + 1
            for half in range(2):
                s = BY[f"att{half}"]
                with dve.Fori(0, 3) as it:
                    ch.start(it, per)
                    group(s, 4 * half, it, None)
                    ch.end(3)
                group(s, 4 * half, 3, BY[f"wo{half}"])
                gemm(f"wo{half}", "m1_1_0" if half else "att1")
            norm_scale(N_MLP1)
            dve.wait_ge(S["kpe_out"], 32)
            for c in range(4):
                gemm(f"m1_1_{c}", f"m2_1_{c}", norm_pair(N_MLP1) if c == 0 else None)
                gemm(f"m2_1_{c}", f"m1_1_{c + 1}" if c < 3 else None)
            norm_scale(N_FIN)
            for b in range(KB):
                nc.vector.scalar_tensor_tensor(out=x[:, b, :], in0=x[:, b, :], scalar=vec[:, G_FIN + b:G_FIN + b + 1],
                                               in1=work[:, 6, :], op0=ALU.mult, op1=ALU.mult).then_inc(y_ready, 1)

        @block.tensor
        def _(pe):
            mm = nc.tensor.matmul

            def ada_slot(s, it, p, n, first):
                pe.wait_ge(lo_ready, s.per * it + (n + 1))
                if p == 0 and not first:
                    pe.wait_ge(arow_ready, s.ada0 + it)
                for j in range(2):
                    for w in (whi, wlo):
                        ins = mm(PS[0:4, 4, :], c4[:, 2 * p + j, :], w[:, n % SPL, 512 * j:512 * j + 512],
                                 start=(p == 0 and j == 0 and w is whi), stop=(p == 7 and j == 1 and w is wlo))
                ins.then_inc(slot_used, 1)

            def ada_finish(g, first=False):
                pe.wait_ge(arow_ready, g + 1)
                if not first:
                    pe.wait_ge(mod_ready, g)
                for m in range(4):
                    ins = mm(PS[:, 5, 2 * m:2 * m + 2], arow[0:4, P * m:P * m + P], con[0:4, SEL:SEL + 2],
                             start=True, stop=True)
                ins.then_inc(ada_fin, 1)

            def three(out, wh, wl, xh, xl, start, stop):
                mm(out, wh, xh, start=start, stop=False)
                mm(out, wl, xh, start=False, stop=False)
                return mm(out, wh, xl, start=False, stop=stop)

            def gemm_slot(s, it, p, n, xh, xl):
                pe.wait_ge(lo_ready, s.per * it + (n + 1))
                if s.src == "A":
                    pe.wait_ge(a_ready, s.a0 + 2 * p + 2)
                else:
                    pe.wait_ge(b_ready, s.hid0 + 2 * p + 2)
                for m in range(4):
                    if p == 0:
                        if s.free0[m] or not isinstance(it, int):
                            pe.wait_ge(bank_free[m], it + s.free0[m])
                    for j in range(2):
                        a = 512 * j + P * m
                        ins = three(PS[:, m, 0:T], whi[:, n % SPL, a:a + P], wlo[:, n % SPL, a:a + P],
                                    xh[:, 2 * p + j, :], xl[:, 2 * p + j, :], p == 0 and j == 0, p == 7 and j == 1)
                    if p == 7 and m < 3:
                        ins.then_inc(gemm_done, 1)
                ins.then_inc(slot_used, 1)

            def gemm(name):
                s = BY[name]
                xh, xl = (ah, al) if s.src == "A" else (bh, bl)

                def group(it):
                    for p in range(8):
                        n = s.n0 + s.wide * p
                        if s.mixed:
                            ada_slot(s, it, p, n, False)
                            n += 1
                        gemm_slot(s, it, p, n, xh, xl)
                    if s.mixed:
                        ada_finish(s.ada0 + it)
                if name == "r":
                    group(0)
                    rounds(pe, 1, 4, group)
                else:
                    rounds(pe, 0, 4, group)

            def mean_square(i, ones):
                for b in range(NORMS[i][0]):
                    pe.wait_ge(sq_ready, SQ0[i] + b + 1)
                    mm(PS[:, 6, 0:T], con[:, ones:ones + P], work[:, b % 2, :], start=b == 0,
                       stop=b == NORMS[i][0] - 1).then_inc(sq_used, 1)

            pe.wait_ge(c4_ready, 1)
            pe.wait_ge(consts_in, 16)
            s = BY["ada0"]
            for p in range(8):
                ada_slot(s, 0, p, p, True)
            ada_finish(0, True)

            def body(it):
                for p in range(8):
                    ada_slot(s, it, p, p, False)
                ada_finish(it)
            rounds(pe, 1, 8, body)
            mean_square(N_MIX0, ONES_D)

            pe.wait_ge(lora1_in, 48)
            for i, (w, parts) in enumerate(((l1w, 1), (l1a, 1), (l1g, 2))):
                m = 96 if i < 2 else P
                for b in range(KB):
                    pe.wait_ge(mix_ready, KB * i + b + 1)
                    for z in range(parts):
                        ins = mm(PS[0:m, i + z, 0:T], w[:, b, P * z:P * z + m], work[:, 2 + b % 2, :],
                                 start=b == 0, stop=b == KB - 1)
                    ins.then_inc(mix_used, 1)
            pe.wait_ge(mids_done, 4)
            gemm("r")
            gemm("k")
            gemm("v")

            pe.wait_ge(bank_free[3], BY["o"].free0[3])

            def body(it):
                top, bot = slice(0, 64), slice(64, 128)
                for u in range(2):
                    t, m = lanes[u], L[u]
                    b0 = 4 * u
                    pe.wait_ge(m["free"], it + 1)
                    pe.wait_ge(m["lane_in"], 48 * it + 48)
                    mm(PS[:, b0, 0:T], t["lw"][0:96, LW_W:LW_W + P], mids[0:96, 0, :], start=True, stop=True)
                    mm(PS[:, b0 + 1, 0:T], t["lw"][0:96, LW_A:LW_A + P], mids[0:96, 1, :], start=True,
                       stop=True).then_inc(m["pre_mm"], 1)
                for u in range(2):
                    t, m = lanes[u], L[u]
                    pe.wait_ge(m["sq"], it + 1)
                    mm(PS[:, 4 * u + 2, 0:TT], con[:, BD1:BD1 + P], t["t2"][:], start=True, stop=True).then_inc(m["pre_mm"], 1)
                for u in range(2):
                    t, m = lanes[u], L[u]
                    b0 = 4 * u
                    pe.wait_ge(m["prep"], it + 1)
                    rb = r[:, bass.ds(2 * it + u, 1), :]
                    for c in range(NCH):
                        tok = slice(C * c, C * c + C)
                        for z, p in ((0, top), (1, bot)):
                            mm(PS[:, b0 + 2 * z, tok], t["bk"][p, c, :], t["wl"][p, z, c, :], start=True, stop=True)
                    for c in range(NCH):
                        tok = slice(C * c, C * c + C)
                        for z, p in ((0, top), (1, bot)):
                            ins = mm(PS[:, b0 + 1 + 2 * z, tok], t["bk"][p, c, :], t["t1"][p, tok], start=True, stop=True)
                    ins.then_inc(m["pre_mm"], 1)
                for u in range(2):
                    t, m = lanes[u], L[u]
                    b0 = 4 * u
                    pe.wait_ge(m["masked"], 6 * it + 6)
                    pe.wait_ge(m["vc"], it + 1)
                    for c in range(NCH):
                        nc.tensor.transpose(PS[:, b0 + c // 4, P * (c % 4):P * (c % 4) + P], t["bk"][:, c, :], ident)
                    for c in range(NCH):
                        tok = slice(C * c, C * c + C)
                        mm(PS[64:128, b0 + 2, tok], t["t5"][:, tok], con[:, IDENT:IDENT + C], start=True, stop=True)
                        mm(PS[0:64, b0 + 2, tok], t["t5"][:, tok], con[:, IDENT + C:IDENT + P], start=True, stop=True)
                    mm(PS[:, b0 + 3, 0:TT], con[:, BD1:BD1 + P], t["t0"][:], start=True, stop=True).then_inc(m["pre_mm"], 1)
                for l in range(LEVELS):
                    for u in range(2):
                        t, m = lanes[u], L[u]
                        if l == 0:
                            pe.wait_ge(m["tokc"], 6 * it + 6)
                        else:
                            pe.wait_ge(m["xu"], (LEVELS - 1) * it + l)
                        for c in range(NCH):
                            tok = slice(C * c, C * c + C)
                            ins = mm(PS[:, 4 * u, tok], t["nbd"][:, c, :], eye2 if l == 0 else t["t3"][:, tok],
                                     start=True, stop=True)
                        ins.then_inc(m["q"], 1)
                    for u in range(2):
                        t, m = lanes[u], L[u]
                        pe.wait_ge(m["qs"], LEVELS * it + l + 1)
                        if 0 < l < LEVELS - 1:
                            pe.wait_ge(m["xtb"], 2 * (LEVELS - 1) * it + 2 * l)
                            for c in range(NCH):
                                tok = slice(C * c, C * c + C)
                                ins = mm(PS[:, 4 * u + 1, tok], t["xbd"][:, c, :], t["t4"][:, tok], start=True, stop=True)
                            ins.then_inc(m["p1"], 1)
                    for u in range(2):
                        t, m = lanes[u], L[u]
                        pe.wait_ge(m["qb"], 2 * LEVELS * it + 2 * l + 2)
                        if l:
                            pe.wait_ge(m["xtu"], (LEVELS - 1) * it + l)
                        for c in range(NCH):
                            tok = slice(C * c, C * c + C)
                            ins = mm(PS[:, 4 * u + 2, tok], t["qbd"][:, c, :], eye2 if l == 0 else t["t5"][:, tok],
                                     start=True, stop=True)
                        ins.then_inc(m["p2"], 1)
                for c in range(NCH):
                    tok = slice(C * c, C * c + C)
                    for u in range(2):
                        t, m = lanes[u], L[u]
                        b0 = 4 * u
                        if c == 0:
                            pe.wait_ge(m["xf"], 2 * it + 2)
                            pe.wait_ge(m["bv"], it + 1)
                        elif c < NCH - 1:
                            pe.wait_ge(m["sn"], 2 * NCH * it + 2 * c)
                        else:
                            pe.wait_ge(m["lane_in"], 48 * it + 48)
                            pe.wait_ge(m["wc"], NCH * it + c)
                        mm(PS[0:64, b0, 0:C], t["wl"][:, 0, c, :], t["sv"][:, 0, c, :], start=True, stop=True)
                        mm(PS[64:128, b0, 0:C], t["wl"][:, 1, c, :], t["sv"][:, 1, c, :], start=True,
                           stop=True).then_inc(m["w"], 1)
                    for u in range(2):
                        t, m = lanes[u], L[u]
                        b0 = 4 * u
                        pe.wait_ge(m["wc"], NCH * it + c + 1)
                        if c:
                            pe.wait_ge(m["uca"], NCH * it + c)
                            pe.wait_ge(m["ucd"], NCH * it + c)
                        mm(PS[:, b0 + 1, 0:C], t["xbd"][:, c, :], t["w"][:], start=True, stop=True).then_inc(m["u"], 1)
                    for u in range(2):
                        t, m = lanes[u], L[u]
                        b0 = 4 * u
                        pe.wait_ge(m["uca"], NCH * it + c + 1)
                        pe.wait_ge(m["ucd"], NCH * it + c + 1)
                        if c:
                            pe.wait_ge(m["sn"], 2 * NCH * it + 2 * c)
                        mm(PS[0:64, b0 + 2, 0:C], t["bk"][:, c, 0:C], t["uv"][:, 0, c, :], start=True, stop=True)
                        mm(PS[64:128, b0 + 2, 0:C], t["bk"][:, c, C:P], t["uv"][:, 1, c, :], start=True,
                           stop=True).then_inc(m["sp"], 1)
                for u in range(2):
                    t, m = lanes[u], L[u]
                    b0 = 4 * u
                    for z, p in ((0, top), (1, bot)):
                        for c in range(NCH):
                            tok = slice(C * c, C * c + C)
                            mm(PS[p, b0 + z, tok], t["sv"][p, z, c, :], t["t1"][p, tok], start=True, stop=False)
                            ins = mm(PS[p, b0 + z, tok], t["uv"][:, z, c, :], t["gr"][:, z, c, :], start=False, stop=True)
                    ins.then_inc(m["post_mm"], 1)
                for u in range(2):
                    t, m = lanes[u], L[u]
                    pe.wait_ge(m["yc"], 2 * it + 2)
                    pe.wait_ge(m["sn"], 2 * NCH * it + 2 * NCH)
                    mm(PS[:, 4 * u + 2, 0:TT], con[:, BD64:BD64 + P], t["t2"][:], start=True, stop=True).then_inc(m["post_mm"], 1)
                for u in range(2):
                    t, m = lanes[u], L[u]
                    pe.wait_ge(m["ys"], it + 1)
                    mm(PS[:, 4 * u + 3, 0:TT], con[:, BD64:BD64 + P], t["t3"][:], start=True, stop=True).then_inc(m["post_mm"], 1)
                for u in range(2):
                    t, m = lanes[u], L[u]
                    mm(PS[:, 4 * u, 0:T], t["lw"][:, LW_G:LW_G + P], mids[:, 2, :], start=True, stop=False)
                    mm(PS[:, 4 * u, 0:T], t["lw"][:, LW_G + P:LW_G + 2 * P], mids[:, 3, :], start=False,
                       stop=True).then_inc(m["post_mm"], 1)
            rounds(pe, 0, KB // 2, body)
            for u in range(2):
                pe.wait_ge(L[u]["free"], KB // 2 + 1)
            gemm("o")
            mean_square(N_MLP0, ONES_D)
            for c in range(4):
                gemm(f"m1_0_{c}")
                gemm(f"m2_0_{c}")
            mean_square(N_KV, ONES_D)

            def four(s, xh, xl, acc):
                for p in range(8):
                    n = s.n0 + p
                    pe.wait_ge(lo_ready, n + 1)
                    pe.wait_ge(a_ready, s.a0 + 2 * p + 2)
                    for m in range(4):
                        if p == 0:
                            pe.wait_ge(bank_free[m], s.free0[m])
                        for j in range(2):
                            a = 512 * j + P * m
                            ins = three(PS[:, m, 0:T], whi[:, n % SPL, a:a + P], wlo[:, n % SPL, a:a + P],
                                        xh[:, 2 * p + j, :], xl[:, 2 * p + j, :], p == 0 and j == 0, p == 7 and j == 1)
                        if p == 7:
                            ins.then_inc(acc, 1)
                    if p < 7:
                        ins.then_inc(slot_used, 1)
            s = BY["kvd"]
            four(s, ah, al, gemm_done)
            pe.wait_ge(gemm_done, s.gd0 + 4)
            pe.sem_inc(slot_used, 1)
            pe.wait_ge(bank_free[0], s.free0[0] + 1)
            for q in range(2):
                n = s.n0 + 8 + q
                pe.wait_ge(lo_ready, n + 1)
                for j in range(8):
                    b = 8 * q + j
                    ins = three(PS[:, 0, 0:T], whi[:, n % SPL, P * j:P * j + P], wlo[:, n % SPL, P * j:P * j + P],
                                ah[:, b, :], al[:, b, :], b == 0, b == KB - 1)
                ins.then_inc(gemm_done if q else slot_used, 1)
            pe.wait_ge(gemm_done, s.gd0 + 5)
            pe.sem_inc(slot_used, 1)
            mean_square(N_LAT, ONES_Q)
            mean_square(N_MIX1, ONES_D)
            pe.wait_ge(S["pe_done"], 2)
            s = BY["wdq"]
            four(s, ah, al, gemm_done)
            pe.wait_ge(gemm_done, s.gd0 + 4)
            pe.sem_inc(slot_used, 1)
            mean_square(N_Q, ONES_Q)
            pe.wait_ge(S["rows_in"], 96)
            pe.wait_ge(S["keys_ready"], 9)
            pe.wait_ge(S["cq_ready"], 4)
            pe.wait_ge(S["pe_done"], 2)
            for m in range(4):
                pe.wait_ge(bank_free[m], BY["wdq"].free0[m] + 1)

            def project(s, it, q0, acc, v4, width, xh, xl, wait):
                for q in range(2):
                    n = s.n0 + q0 + q
                    pe.wait_ge(lo_ready, s.per * it + (n + 1))
                    for m in range(4):
                        if q == 0:
                            wait(m)
                        for j in range(2):
                            a = 512 * j + P * m
                            ins = three(PS[:, m, 0:width], whi[:, n % SPL, a:a + P], wlo[:, n % SPL, a:a + P],
                                        xh[:, 2 * q + j, :], xl[:, 2 * q + j, :], q == 0 and j == 0, q == 1 and j == 1)
                        if q == 1:
                            ins.then_inc(acc, 1)
                    if q == 0:
                        ins.then_inc(slot_used, 1)
                pe.wait_ge(acc, v4 + 4)
                pe.sem_inc(slot_used, 1)

            def group(s, g0, it):
                v1, v4 = it + (g0 + 1), it * 4 + 4 * g0

                def after_group(m):
                    if g0 == 0 and isinstance(it, int) and it == 0:
                        return
                    if m == 0:
                        pe.wait_ge(S["pts_done"], 2 * it + 2 * g0)
                    elif m < 3:
                        pe.wait_ge(S["pt_done"], v4)
                    if g0 == 4:
                        pe.wait_ge(bank_free[m], s.free0[m])
                project(s, it, 0, S["kt_acc"], v4, KEYS, kyh, kyl, after_group)
                for q in range(2):
                    n = s.n0 + 2 + q
                    pe.wait_ge(lo_ready, s.per * it + (n + 1))
                    for m in range(4):
                        w = P if m < 3 else TS
                        if q == 0:
                            pe.wait_ge(S["kt_done"], v4 + m + 1)
                        for j in range(2):
                            cols = slice(P * m, P * m + w)
                            kb = 2 * q + j
                            o, wa = PS[0:w, m, :], slice(512 * j, 512 * j + 512)
                            mm(o, kyh[:, kb, cols], whi[:, n % SPL, wa], start=kb == 0, stop=False)
                            mm(o, kyl[:, kb, cols], whi[:, n % SPL, wa], start=False, stop=False)
                            ins = mm(o, kyh[:, kb, cols], wlo[:, n % SPL, wa], start=False, stop=kb == 3)
                        if q == 1:
                            ins.then_inc(S["v_acc"], 1)
                    if q == 0:
                        ins.then_inc(slot_used, 1)
                pe.wait_ge(S["v_acc"], v4 + 4)
                pe.sem_inc(slot_used, 1)
                project(s, it, 4, S["qn_acc"], v4, T, cqh, cql, lambda m: pe.wait_ge(S["v_done"], v4 + m + 1))
                project(s, it, 6, S["qr_acc"], v4, T, cqh, cql, lambda m: pe.wait_ge(S["qn_done"], v4 + m + 1))
                for h in range(4):
                    pe.wait_ge(S["qr_done"], v4 + h + 1)
                    for a, b, qc, kc in ((0, P, slice(0, P), slice(0, P)), (P, 384, slice(P, TP), slice(0, TP))):
                        mm(PS[:, 4 + h, a:b], qn[:, h, qc], kt[:, h, kc], start=True, stop=False)
                        mm(PS[:, 4 + h, a:b], qp[0:66, h, qc], kpe[0:66, kc], start=False, stop=True)
                for h in range(4):
                    if h == 0:
                        pe.wait_ge(S["qr_done"], v4 + 4)
                    o = PS[32 * h:32 * h + 32, 0, 0:SK]
                    mm(o, qn[:, h, TP:T], kt[:, h, TP:KEYS], start=True, stop=False)
                    ins = mm(o, qp[0:66, h, TP:T], kpe[0:66, TP:KEYS], start=False, stop=True)
                ins.then_inc(S["s_acc"], 1)
                pe.wait_ge(S["nrmd"], 3 * v1 - 2)
                nc.tensor.transpose(PS[:, 0, 0:P], prs[:, 0:P], ident)
                nc.tensor.transpose(PS[0:32, 0, P:2 * P], prs[:, P:SK], ident).then_inc(S["pts_acc"], 1)
                pe.wait_ge(S["nrmd"], 3 * v1)

                def turn(h):
                    if h >= 2:
                        pe.wait_ge(S["pt_done"], v4 + h - 1)
                    for c in range(3):
                        ins = nc.tensor.transpose(PS[:, 1 + h % 2, P * c:P * c + P], pr[:, h, P * c:P * c + P], ident)
                    ins.then_inc(S["pt_acc"], 1)

                def values(h):
                    hd = slice(P * h, P * h + P)
                    pe.wait_ge(S["pt_done"], v4 + h + 1)
                    if h == 0:
                        pe.wait_ge(S["pts_done"], 2 * v1)
                    mm(PS[:, 4 + h, 0:TP], vt[:, 0, hd], pt[:, h % 2, 0:TP], start=True, stop=False)
                    mm(PS[:, 4 + h, P:TP], vt[:, 1, hd], pt[:, h % 2, TP:384], start=False, stop=True)
                    mm(PS[:, 4 + h, TP:T], vt[:, 2, hd], pts[:, 0, 32 * h:32 * h + 32], start=True, stop=False)
                    mm(PS[:, 4 + h, TP:T], vt[0:32, 3, hd], pts[0:32, 1, 32 * h:32 * h + 32], start=False,
                       stop=True).then_inc(S["o_acc"], 1)
                turn(0)
                turn(1)
                for h in range(4):
                    values(h)
                    if h < 2:
                        turn(h + 2)

            for half in range(2):
                s = BY[f"att{half}"]
                if half == 0:
                    group(s, 0, 0)
                rounds(pe, 1 - half, 4, lambda it: group(s, 4 * half, it))
                pe.wait_ge(S["pts_done"], 8 * half + 8)
                pe.wait_ge(S["pt_done"], 16 * half + 16)
                gemm(f"wo{half}")
            mean_square(N_MLP1, ONES_D)
            for c in range(4):
                gemm(f"m1_1_{c}")
                gemm(f"m2_1_{c}")
            mean_square(N_FIN, ONES_D)


def halves(w):
    kk, m = w.shape
    a = w.reshape(kk // 256, 2, P, m // 512, 512).transpose(3, 0, 2, 1, 4)
    return a.reshape(-1, P, HS)


def woven(a, b):
    return np.stack([a, b], 1).reshape(-1, P, HS)


def column(a):
    return np.asarray(a).reshape(-1, P).T


def tokens(p, s):
    a = np.concatenate([p, s], 0)
    return np.ascontiguousarray(a.T.reshape(-1, P, a.shape[0]).transpose(1, 0, 2))


def constants():
    c = np.zeros((P, NCONST), np.float32)
    p, t = np.arange(P)[:, None], np.arange(C)[None, :]
    c[:, IDENT:IDENT + P] = np.eye(P)
    c[:, ONES_D:ONES_D + P] = 1.0 / D
    c[:, ONES_Q:ONES_Q + P] = 1.0 / KV
    same = (p // C) == (np.arange(P)[None, :] // C)
    c[:, BD1:BD1 + P] = same
    c[:, BD64:BD64 + P] = same / C
    i = p % C
    c[:, MASK_S:MASK_S + C] = i < t
    c[:, MASK_I:MASK_I + C] = i <= t
    for l in range(LEVELS):
        c[:, MASK_L + C * l:MASK_L + C * l + C] = ((i >> (l + 1)) == (t >> (l + 1))) & ((i >> l) % 2 == 1) & ((t >> l) % 2 == 0)
    c[:, EYE2:EYE2 + C] = i == t
    c[:, CARRY:CARRY + TT] = np.arange(TT)[None, :] % C != 0
    for q in range(4):
        c[q, SEL + q % 2] = 1.0
    return c


def rotary():
    half = ROPE // 2
    inv = np.float32(10000.0) ** (-np.arange(half, dtype=np.float32) / np.float32(half))
    pos = np.concatenate([np.arange(TP), PAST + np.arange(TS)]).astype(np.float32)
    ang = (inv[:, None] * pos[None, :]).astype(np.float32)
    cos, sin = np.cos(ang), np.sin(ang)
    return np.concatenate([cos, cos, -sin, sin], 0).astype(np.float32)


def swapped(w):
    return np.concatenate([w, w[..., ROPE // 2:], w[..., :ROPE // 2]], -1)


def kernel(**inputs):
    import concourse.bacc as bacc
    from concourse.bass_utils import run_bass_kernel_spmd

    a = {n: np.asarray(z) for n, z in inputs.items()}
    f = np.float32
    ada = [a["ada_w"][0], a["ada_w"][1], a["kv_ada_w"]]
    own = halves(ada[0])
    later = np.concatenate([halves(ada[1]), halves(ada[2])], 0)
    parts = [own[:64]]
    for i, n in enumerate(("rw_wr", "rw_wk", "rw_wv", "rw_wo")):
        parts.append(woven(own[64 + 32 * i:96 + 32 * i], halves(a[n][0])))
    for layer in range(2):
        for c in range(4):
            cols = slice(D * c, D * c + D)
            for j, w in enumerate((a["mlp_w1"][layer][:, cols], a["mlp_w2"][layer][cols])):
                h = halves(w)
                g = 32 * (2 * c + j)
                parts.append(woven(later[g:g + 32], h) if layer == 0 else h)
        if layer:
            break
        parts.append(halves(a["kv_wd"][:, :KV]))
        pe = swapped(a["kv_wd"][:, KV:])
        parts.append(pe.reshape(2, 8, P, P).transpose(0, 2, 1, 3).reshape(2, P, HS))
        parts.append(halves(a["mla_wdq"][0]))
        wq = a["mla_wuq"][0].reshape(KV, HEADS, NOPE + ROPE)
        per = [halves(a["kv_wuk"].reshape(KV, -1)), halves(a["kv_wuv"].reshape(KV, -1)),
               halves(np.ascontiguousarray(wq[..., :NOPE]).reshape(KV, -1)), halves(swapped(wq[..., NOPE:]).reshape(KV, -1))]
        per = np.stack([z.reshape(8, 2, P, HS) for z in per], 1).reshape(8, 8, P, HS)
        for half in range(2):
            parts.append(per[4 * half:4 * half + 4].reshape(-1, P, HS))
            parts.append(halves(a["mla_wo"][0][D * half:D * half + D]))
    stream = np.concatenate(parts, 0)

    vec = np.concatenate([column(z) for z in (
        a["ada_b"][0], a["ada_b"][1], a["kv_ada_b"], a["norm_mix_g"][0], a["norm_mlp_g"][0], a["norm_mix_g"][1],
        a["norm_mlp_g"][1], a["kv_norm_g"], a["final_g"], a["rw_mu"][0].reshape(-1), a["state_shift"][0, 0],
        a["kv_lat_g"], a["mla_q_g"][0])], 1)
    lw = np.zeros((KB, P, NLW), f)
    for i, w in enumerate((a["rw_w2"][0], a["rw_a2"][0])):
        lw[:, 0:96, P * i:P * i + P] = w.reshape(96, KB, P).transpose(1, 0, 2)
    g2 = a["rw_g2"][0].reshape(2, P, KB, P)
    for i in range(2):
        lw[:, :, LW_G + P * i:LW_G + P * i + P] = g2[i].transpose(1, 0, 2)
    for i, n in enumerate(("rw_w0", "rw_a0", "rw_kk", "rw_ka", "rw_rk", "rw_lnx_g", "rw_lnx_b")):
        lw[:, :, LW_P + i] = a[n][0].reshape(KB, P)
    s0 = a["state_wkv"][0, 0].transpose(0, 2, 1).reshape(KB, P, C)
    krow = np.zeros((2, KEYS), f)
    qrow = np.zeros((2, T), f)
    for i in range(2):
        krow[i, P * i + C:P * i + 2 * C] = -1e30
        qrow[i, P * i:P * i + C] = 1.0

    ins = {
        "stream": stream, "xT": tokens(a["x_prompt"][0], a["x_sample"][0]),
        "cT": np.stack([column(a["c_prompt"][0]), column(a["c_sample"][0])], -1),
        "con": constants(), "vec": vec, "lw": lw, "s0": s0,
        "l1w": a["rw_w1"][0].reshape(KB, P, 96).transpose(1, 0, 2),
        "l1a": a["rw_a1"][0].reshape(KB, P, 96).transpose(1, 0, 2),
        "l1g": a["rw_g1"][0].reshape(KB, P, 256).transpose(1, 0, 2),
        "trig": rotary(), "krow": krow, "qrow": qrow,
        "cckv": a["cache_ckv"][0].T.reshape(4, P, PAST).transpose(1, 0, 2), "ckpe": a["cache_kpe"][0].T,
    }
    outs = {"yT": (P, KB, T), "ckvT": (P, 4, T), "kpeT": (ROPE, T), "wkvT": (KB, P, 2, C), "shiftT": (P, 2, KB)}
    nc = bacc.Bacc("TRN2", target_bir_lowering=False, num_devices=1)
    d = {}
    for n in ins:
        ins[n] = np.ascontiguousarray(ins[n])
        d[n] = nc.dram_tensor(n, ins[n].shape, F32, kind="ExternalInput").ap()
    for n, shape in outs.items():
        d[n] = nc.dram_tensor(n, shape, F32, kind="ExternalOutput").ap()
    trunk(nc, d)
    got = run_bass_kernel_spmd(nc, [ins], core_ids=[0]).results[0]

    def rows(z, n):
        return z.transpose(2, 1, 0).reshape(T, n * P)

    y, ckv, kpe = rows(got["yT"], KB), rows(got["ckvT"], 4), got["kpeT"].T
    wkv = got["wkvT"].reshape(KB, 2, C, 2, C).transpose(3, 0, 1, 4, 2).reshape(2, 1, 1, HEADS, C, C)
    shift = got["shiftT"].transpose(1, 2, 0).reshape(2, 1, 1, D)
    return tuple(np.ascontiguousarray(z) for z in (
        y[None, :TP], y[None, TP:], ckv[None, :TP], kpe[None, :TP], wkv[0], shift[0],
        ckv[None, TP:], kpe[None, TP:], wkv[1], shift[1]))
```

```python
from contextlib import ExitStack

import numpy as np
import concourse.bass as bass
from concourse import mybir

F32 = mybir.dt.float32
F32R = mybir.dt.float32r
ALU = mybir.AluOpType
ACT = mybir.ActivationFunctionType
AX = mybir.AxisListType

P = 128
D = 2048
KB = D // P
TP, TS = 256, 32
T = TP + TS
C = 64
NCH = TP // C + 1
TT = NCH * C
PAST = 128
KEYS = TP + PAST + TS
SK = PAST + TS
HEADS = 32
KV = 512
NOPE, ROPE, VD = 128, 64, 128
SCALE = float((NOPE + ROPE) ** -0.5)
EPS = 1e-6
GN_EPS = 64e-5
HS = 1024
RAW, SPL = 8, 4
LEVELS = 6
DEC = float(np.exp(-0.5))

ADAB = 0
MOD_BLOCKS = 2 * 6 * KB + 2 * KB
G_MIX0, G_MLP0, G_MIX1, G_MLP1, G_KV, G_FIN = [MOD_BLOCKS + KB * i for i in range(6)]
MU = G_FIN + KB
SHIFT = MU + 6 * KB
LATG = SHIFT + KB
QG = LATG + 4
NVEC = QG + 4
IDENT, ONES_D, ONES_Q, BD1, BD64 = [P * i for i in range(5)]
MASK_S = 5 * P
MASK_I = MASK_S + C
MASK_L = MASK_I + C
EYE2 = MASK_L + LEVELS * C
CARRY = EYE2 + C
SEL = CARRY + TT
NCONST = SEL + 2
LW_W, LW_A, LW_G, LW_P = 0, P, 2 * P, 4 * P
PW0, PA0, PKK, PKA, PRK, PLG, PLB = range(LW_P, LW_P + 7)
NLW = 4 * P + 8
Z, SSQ, GRAM, TOK = range(1, 5)
Y, MEAN, VAR, GATE = range(1, 5)
SCAN_CHAIN = 2 * (2 + 13 + 1 + 4)


class Stage:

    def __init__(self, name, groups, per, mixed=False, epi=None, src=None, gate=None):
        self.name, self.groups, self.per = name, groups, per
        self.mixed, self.epi, self.src, self.gate = mixed, epi, src, gate
        self.wide = 2 if self.mixed else 1
        self.hoist = 3 if self.mixed else 2

    def ada_slot(self, j):
        return self.name == "ada0" or (self.mixed and j % 2 == 0)


def plan():
    st = [Stage("ada0", 8, 8)]
    for n in ("r", "k", "v"):
        st.append(Stage(n, 4, 16, mixed=True, epi="copy", src="A"))
    st.append(Stage("o", 4, 16, mixed=True, epi="resid", src="A", gate=2))
    for c in range(4):
        st.append(Stage(f"m1_0_{c}", 4, 16, mixed=True, epi="relu2", src="A"))
        st.append(Stage(f"m2_0_{c}", 4, 16, mixed=True, epi="resid", src="B", gate=5))
    st.append(Stage("kvd", 1, 10, src="A"))
    st.append(Stage("wdq", 1, 8, src="A"))
    st.append(Stage("att0", 4, 8))
    st.append(Stage("wo0", 4, 8, epi="resid", src="A", gate=8))
    st.append(Stage("att1", 4, 8))
    st.append(Stage("wo1", 4, 8, epi="resid", src="A", gate=8))
    for c in range(4):
        st.append(Stage(f"m1_1_{c}", 4, 8, epi="relu2", src="A"))
        st.append(Stage(f"m2_1_{c}", 4, 8, epi="resid", src="B", gate=11))
    n = ada = gd = hidden = 0
    free = [0] * 4
    makers = ["r", "k", "v", "o", "m1_0_0", "kvd", "wdq", "wo0", "wo1", "m1_1_0"]
    a0 = 0
    for s in st:
        s.n0, s.ada0, s.gd0, s.free0, s.hid0 = n, ada, gd, list(free), hidden
        n += s.groups * s.per
        if s.mixed or s.name == "ada0":
            ada += s.groups
        if s.name in makers:
            a0 = KB * makers.index(s.name)
        s.a0 = a0
        if s.name == "kvd":
            gd, free = gd + 5, [f + 1 for f in free]
        elif s.name == "wdq":
            gd, free = gd + 4, [f + 1 for f in free]
        elif s.epi:
            gd, free = gd + 3 * 4, [f + 4 for f in free]
        if s.epi == "relu2":
            hidden += KB
        if s.src == "B":
            s.hid0 -= KB
    return st, n, free


ST, NSLOTS, FREE_END = plan()
BY = {s.name: s for s in ST}
NORMS = [(KB, 0), (KB, BY["m1_0_0"].free0[3]), (KB, BY["kvd"].free0[3]), (4, 0), (KB, 0), (4, 0),
         (KB, BY["m1_1_0"].free0[3]), (KB, FREE_END[3])]
N_MIX0, N_MLP0, N_KV, N_LAT, N_MIX1, N_Q, N_MLP1, N_FIN = range(8)
SQ0 = [sum(n for n, _ in NORMS[:i]) for i in range(9)]
MODULATED = {N_MIX0: 0, N_MLP0: 1, N_KV: 2, N_MIX1: 3, N_MLP1: 4}
NORM_MOD = {N_MIX0: (0, KB, G_MIX0, 8, None), N_MLP0: (3 * KB, 4 * KB, G_MLP0, 20, "m1_0_0"),
            N_KV: (12 * KB, 13 * KB, G_KV, 56, "kvd"), N_MIX1: (6 * KB, 7 * KB, G_MIX1, 56, "wdq"),
            N_MLP1: (9 * KB, 10 * KB, G_MLP1, 56, "m1_1_0")}


def addr_plan():
    sizes = [("RAW", RAW * HS * 4), ("HI", SPL * HS * 4), ("LO", SPL * HS * 4), ("AH", KB * T * 4),
             ("AL", KB * T * 4), ("R", KB * TT * 4), ("K", KB * TT * 4), ("V", KB * TT * 4),
             ("H", KB * (T + 2) * 4 + 32), ("WORK", 7 * T * 4), ("SPARE", 3072), ("CONST", NCONST * 4 + 24),
             ("VEC", NVEC * 4 + 32), ("MOD", MOD_BLOCKS * 8), ("SMALL", 1024), ("MIDS", 4 * T * 4)]
    at, out = 16512, {}
    for n, s in sizes:
        at = (at + 31) // 32 * 32
        out[n] = at
        at += s
    out["END"] = at
    assert at <= 229344, at
    return out


class Count:

    def __init__(self, eng, sem):
        self.eng, self.sem, self.n, self.off = eng, sem, 0, 0

    def inc(self, ins):
        ins.then_inc(self.sem, 1)
        self.n += 1
        return ins

    def wait(self):
        self.eng.wait_ge(self.sem, self.off + self.n)

    def start(self, it, per):
        self.n0, self.per, self.off = self.n, per, it * per

    def end(self, rounds):
        assert self.n - self.n0 == self.per, (self.n - self.n0, self.per)
        self.n, self.off = self.n0 + self.per * rounds, 0


def trunk(nc, d):
    es = ExitStack()
    at = addr_plan()

    def sb(name, shape, region, off=0, dt=F32):
        return nc.alloc_sbuf_tensor_at("sb_" + name, shape, dt, offset=at[region] + off)

    def sem(name):
        return es.enter_context(nc.semaphore("sem_" + name))

    with es:
        PS = es.enter_context(nc.psum_tensor("ps", [P, 8, 512], F32))
        raw = sb("raw", [P, RAW, HS], "RAW")
        whi = sb("whi", [P, SPL, HS], "HI", dt=F32R)
        wf = sb("wf", [P, SPL, HS], "HI")
        wlo = sb("wlo", [P, SPL, HS], "LO", dt=F32R)
        ah = sb("ah", [P, KB, T], "AH", dt=F32R)
        al = sb("al", [P, KB, T], "AL", dt=F32R)
        x = sb("x", [P, KB, T], "R")
        r = sb("r", [P, KB, TT], "R")
        k = sb("k", [P, KB, TT], "K")
        v = sb("v", [P, KB, TT], "V")
        bh = sb("bh", [P, KB, T], "K", dt=F32R)
        bl = sb("bl", [P, KB, T], "K", KB * T * 4, dt=F32R)
        hb = sb("hb", [P, KB, T + 2], "H")
        work = sb("work", [P, 7, T], "WORK")
        arow = sb("arow", [P, 512], "SPARE")
        con = sb("con", [P, NCONST], "CONST")
        vec = sb("vec", [P, NVEC], "VEC")
        mod = sb("mod", [P, MOD_BLOCKS, 2], "MOD")
        gs = sb("gs", [P, KB, 2], "SMALL")
        cs = sb("cs", [P, KB, 2], "SMALL", 128)
        csg = sb("csg", [P, KB, 2], "SMALL", 256)
        eps = sb("eps", [P, 2], "SMALL", 384)
        last = sb("last", [P, 2, KB], "SMALL", 416)
        mxs = sb("mxs", [P, 9], "SMALL", 544)
        sms = sb("sms", [P, 9], "SMALL", 608)
        rsm = sb("rsm", [P, 9], "SMALL", 672)
        mids = sb("mids", [P, 4, T], "MIDS")
        l1w = sb("l1w", [P, KB, 96], "K")
        l1a = sb("l1a", [P, KB, 96], "K", KB * 96 * 4)
        l1g = sb("l1g", [P, KB, 256], "K", 2 * KB * 96 * 4)

        lanes = []
        for u in range(2):
            region, off = ("HI", "H")[u], 0
            t = {}
            for name, shape in ([("lw0", [P, NLW]), ("lw1", [P, NLW])] + [(f"t{i}", [P, TT]) for i in range(6)]
                                + [("e", [P, NCH, C + 1]), ("bk", [P, NCH, P]), ("nd", [P, NCH, C]),
                                   ("wl", [P, NCH, 3, C])]
                                + [(n, [P, 2, NCH, C]) for n in ("sv", "uv", "gr")]
                                + [("w", [P, C]), ("sd", [P, C]), ("st", [P, 2, C])]):
                t[name] = sb(f"{name}{u}", shape, region, off)
                size = 4
                for z in shape[1:]:
                    size *= z
                off += (size + 31) // 32 * 32
            limit = (at["AH"] - at["HI"], at["CONST"] - at["H"])[u]
            assert off <= limit, (off, limit)
            lanes.append(t)

        def att(name, shape, dt=F32, state={"off": 0}):
            out = nc.alloc_sbuf_tensor_at("sb_" + name, shape, dt, offset=at["K"] + state["off"])
            size = 4
            for z in shape[1:]:
                size *= z
            state["off"] += (size + 31) // 32 * 32
            assert at["K"] + state["off"] <= at["WORK"], name
            return out

        kyh = att("kyh", [P, 4, KEYS], F32R)
        kyl = att("kyl", [P, 4, KEYS], F32R)
        kpe = att("kpe", [66, KEYS])
        cqh = att("cqh", [P, 4, T], F32R)
        cql = att("cql", [P, 4, T], F32R)
        kt = att("kt", [P, 4, KEYS])
        vt = att("vt", [P, 4, 512])
        qn = att("qn", [P, 4, T])
        qp = att("qp", [66, 4, T])
        pr = att("pr", [P, 4, 384])
        pt = att("pt", [P, 2, 384])
        trig = sb("trig", [P, T], "MIDS")
        prs = sb("prs", [P, SK], "MIDS", T * 4)
        pts = sb("pts", [P, 2, P], "MIDS", T * 4 + SK * 4)
        lat = kt
        cache = vt

        ident = con[:, IDENT:IDENT + P]
        mask_s = con[:, MASK_S:MASK_S + C]
        mask_i = con[:, MASK_I:MASK_I + C]
        eye2 = con[:, EYE2:EYE2 + C]

        landed = [sem(f"landed{i}") for i in range(RAW)]
        hi_ready, lo_ready, slot_used = sem("hi_ready"), sem("lo_ready"), sem("slot_used")
        gemm_done = sem("gemm_done")
        bank_free = [sem(f"bank_free{i}") for i in range(4)]
        arow_ready, ada_fin, mod_ready = sem("arow_ready"), sem("ada_fin"), sem("mod_ready")
        consts_in, vec_in, c_in, x_in, lora1_in, y_out = (
            sem(n) for n in ("consts_in", "vec_in", "c_in", "x_in", "lora1_in", "y_out"))
        c_sig, silu_ready, eps_ready = sem("c_sig"), sem("silu_ready"), sem("eps_ready")
        a_ready, b_ready, sqhi_done = sem("a_ready"), sem("b_ready"), sem("sqhi_done")
        dve_chain, hid_sq = sem("dve_chain"), sem("hid_sq")
        sq_ready, sq_used, root_done, scaled, mod_done, nhi_done, gs_done = (
            sem(n) for n in ("sq_ready", "sq_used", "root_done", "scaled", "mod_done", "nhi_done", "gs_done"))
        mix_ready, mix_used, mixhi_done, mids_done = (
            sem(n) for n in ("mix_ready", "mix_used", "mixhi_done", "mids_done"))
        last_ready, last_out = sem("last_ready"), sem("last_out")
        lane_sems = ("lw0 lw1 s0 vc pre_mm sg sq cum ex nrm prep masked tokc bv q qs p1 p2 xu xtu w wc u uca ucd "
                     "sp sd sn yc yd ys vs post_mm yg oh free sto").split()
        L = [{n: sem(f"{n}_{u}") for n in lane_sems} for u in range(2)]
        att_sems = ("cache_in trig_in rows_in keys_hi keys_ready cachehi pe_done lat_scaled cqhi cq_ready "
                    "kt_acc kt_done v_acc v_done qn_acc qn_done qr_acc qr_done s_acc nmx ex nrmd "
                    "pt_acc pt_done pts_acc pts_done o_acc ohi kpe_out ckv_out").split()
        S = {n: sem("at_" + n) for n in att_sems}
        quarters = sem("quarters")
        rows_zeroed = sem("rows_zeroed")
        y_ready, x_back = sem("y_ready"), sem("x_back")

        block = es.enter_context(nc.Block())

        def rounds(eng, first, end, body):
            if end - first == 1:
                body(first)
            elif end > first:
                with eng.Fori(first, end) as it:
                    body(it)

        def flat(ap):
            return ap.rearrange("p a t -> p (a t)")

        def bank_wait(eng, s, it, m):
            if m < 3:
                eng.wait_ge(gemm_done, 3 * it + (s.gd0 + m + 1))
            else:
                eng.wait_ge(slot_used, s.per * it + (s.n0 + s.per))

        def reader_done(eng, s, p):
            eng.wait_ge(slot_used, s.n0 + (s.groups - 1) * s.per + s.wide * (p + 1))

        def walk(eng, s, nxt, split, produce, epi, row, mods):
            def group(it, after, make=None):
                if make is None:
                    for j in range(s.hoist, s.per):
                        split(s, j, it)
                else:
                    for p in range(KB // 2):
                        make(p)
                        for j in range(s.wide * p + s.hoist, min(s.wide * (p + 1) + s.hoist, s.per)):
                            split(s, j, it)
                if s.mixed:
                    row(s, it)
                if after is not None:
                    for j in range(after.hoist):
                        if j == after.hoist - 1:
                            epi(s, it, (0,))
                        split(after, (s.per if after is s else 0) + j, it if after is s else 0)
                    epi(s, it, (1, 2, 3))
                else:
                    epi(s, it, (0, 1, 2, 3))
                if s.mixed:
                    mods(s.ada0 + it)

            if produce is not None:
                group(0, s, produce)
            rounds(eng, 0 if produce is None else 1, 3, lambda it: group(it, s))
            group(3, BY[nxt] if nxt else None)

        def no(*_):
            pass

        @block.sync
        def _(sp):
            sp.dma_start(csg[:], d["cT"]).then_inc(c_in, 16)
            sp.dma_start(con[:], d["con"]).then_inc(consts_in, 16)
            sp.dma_start(vec[:], d["vec"]).then_inc(vec_in, 16)
            for n in range(RAW):
                sp.dma_start(raw[:, n, :], d["stream"][n]).then_inc(landed[n], 16)
            sp.dma_start(x[:], d["xT"]).then_inc(x_in, 16)
            sp.dma_start(l1w[:], d["l1w"]).then_inc(lora1_in, 16)
            sp.dma_start(l1a[:], d["l1a"]).then_inc(lora1_in, 16)
            sp.dma_start(l1g[:], d["l1g"]).then_inc(lora1_in, 16)
            with sp.Fori(1, NSLOTS // RAW) as i:
                for q in range(RAW):
                    sp.wait_ge(lo_ready, i * RAW + (q + 1 - RAW))
                    sp.dma_start(raw[:, q, :], d["stream"][bass.ds(i * RAW + q, 1)].rearrange("a p c -> (a p) c")
                                 ).then_inc(landed[q], 16)
            for n in range(NSLOTS // RAW * RAW, NSLOTS):
                sp.wait_ge(lo_ready, n + 1 - RAW)
                sp.dma_start(raw[:, n % RAW, :], d["stream"][n]).then_inc(landed[n % RAW], 16)
            sp.wait_ge(y_ready, KB)
            sp.dma_start(d["yT"], x[:]).then_inc(y_out, 16)
            sp.wait_ge(y_out, 16)

        @block.gpsimd
        def _(pool):
            pool.wait_ge(last_ready, 1)
            pool.dma_start(d["shiftT"], last[:]).then_inc(last_out, 16)

            def load_lw(u, blk, h):
                pool.dma_start(lanes[u][f"lw{h}"][:], d["lw"][bass.ds(2 * blk + u, 1)].rearrange("a p c -> (a p) c")
                               ).then_inc(L[u][f"lw{h}"], 16)

            def block_io(blk, h, more=True):
                for u in range(2):
                    t, m = lanes[u], L[u]
                    pool.wait_ge(m["free"], blk + 1)
                    if more:
                        load_lw(u, blk + 1, 1 - h)
                    for z in range(2):
                        p = slice(64 * z, 64 * z + 64)
                        pool.dma_start(t["sv"][p, z, NCH - 1, :],
                                       d["s0"][bass.ds(2 * blk + u, 1), p].rearrange("a p c -> (a p) c")
                                       ).then_inc(m["s0"], 16)
                for u in range(2):
                    t, m = lanes[u], L[u]
                    pool.wait_ge(m["sn"], 2 * NCH * blk + 2 * NCH)
                    pool.dma_start(d["wkvT"][bass.ds(2 * blk + u, 1)].rearrange("a p s c -> (a p) s c"), t["st"][:]
                                   ).then_inc(m["sto"], 16)
                    pool.wait_ge(m["sto"], 16 * blk + 16)
            for u in range(2):
                pool.wait_ge(L[u]["free"], 1)
                load_lw(u, 0, 0)
            rounds(pool, 0, KB // 4 - 1, lambda it: [block_io(2 * it + h, h) for h in range(2)])
            block_io(KB // 2 - 2, 0)
            block_io(KB // 2 - 1, 1, False)
            for u in range(2):
                pool.wait_ge(L[u]["free"], KB // 2 + 1)
            pool.dma_start(x[:], d["xT"]).then_inc(x_back, 16)
            pool.dma_start(trig[:], d["trig"]).then_inc(S["trig_in"], 16)
            pool.wait_ge(slot_used, BY["kvd"].n0)
            pool.dma_start(cache[:, :, 0:PAST], d["cckv"]).then_inc(S["cache_in"], 16)
            pool.dma_start(kpe[0:64, TP:TP + PAST], d["ckpe"]).then_inc(S["rows_in"], 16)
            pool.dma_start(kpe[64:66, :], d["krow"]).then_inc(S["rows_in"], 16)
            for h in range(4):
                pool.dma_start(qp[64:66, h, :], d["qrow"]).then_inc(S["rows_in"], 16)
            pool.wait_ge(S["lat_scaled"], 4)
            pool.dma_start(d["ckvT"], lat[:, :, 0:T]).then_inc(S["ckv_out"], 16)
            pool.wait_ge(S["pe_done"], 2)
            pool.dma_start(d["kpeT"][:, 0:TP], kpe[0:64, 0:TP]).then_inc(S["kpe_out"], 16)
            pool.dma_start(d["kpeT"][:, TP:T], kpe[0:64, TP + PAST:KEYS]).then_inc(S["kpe_out"], 16)
            pool.wait_ge(last_out, 16)
            pool.wait_ge(S["ckv_out"], 16)
            pool.wait_ge(S["kpe_out"], 32)

        @block.scalar
        def _(act):
            def split(s, j, it=0):
                n, step = s.n0 + j, it * s.per
                act.wait_ge(landed[n % RAW], step * 2 + 16 * (n // RAW + 1))
                if n >= SPL or not isinstance(it, int):
                    act.wait_ge(slot_used, step + (n - SPL + 1))
                dst = wf if s.ada_slot(j) else whi
                nc.scalar.activation(dst[:, n % SPL, :], raw[:, n % RAW, :], ACT.Copy).then_inc(hi_ready, 1)

            def epi(s, it, banks):
                if s.epi == "copy":
                    dst = {"r": r, "k": k, "v": v}[s.name]
                    for m in banks:
                        bank_wait(act, s, it, m)
                        nc.scalar.activation(flat(dst[:, bass.ds(4 * it + m, 1), 0:T]),
                                             PS[:, m, 0:T], ACT.Copy).then_inc(bank_free[m], 1)
                elif s.epi == "relu2":
                    for m in banks:
                        i = s.hid0 + m
                        bank_wait(act, s, it, m)
                        if i >= 2:
                            act.wait_ge(b_ready, 4 * it + (i - 1))
                        nc.scalar.activation(work[:, m % 2, :], PS[:, m, 0:T], ACT.Relu).then_inc(bank_free[m], 1)
                        act.wait_ge(bank_free[m], it + (s.free0[m] + 1))
                        nc.scalar.activation(flat(bh[:, bass.ds(4 * it + m, 1), :]),
                                             work[:, m % 2, :], ACT.Square).then_inc(sqhi_done, 1)

            def gemm(name, nxt, produce=None):
                walk(act, BY[name], nxt, split, produce, epi, no, no)

            def norm_root(i, src):
                nb, need = NORMS[i]
                if i == N_MIX0:
                    act.wait_ge(x_in, 16)
                elif need:
                    act.wait_ge(bank_free[3], need)
                for b in range(nb):
                    q = SQ0[i] + b
                    if q >= 2:
                        act.wait_ge(sq_used, q - 1)
                    if i == N_LAT:
                        act.wait_ge(bank_free[b], BY["kvd"].free0[b] + 1)
                    if i == N_Q:
                        act.wait_ge(bank_free[b], BY["wdq"].free0[b] + 1)
                    nc.scalar.activation(work[:, b % 2, :], src[:, b, 0:T], ACT.Square).then_inc(sq_ready, 1)
                act.wait_ge(sq_used, SQ0[i + 1])
                nc.scalar.activation(work[:, 6, :], PS[:, 6, 0:T], ACT.Sqrt, bias=eps[:, 0:1]).then_inc(root_done, 1)

            def modulate(i, b, to_h):
                q = KB * MODULATED[i] + b
                sh = NORM_MOD[i][0]
                if b == 0:
                    act.wait_ge(gs_done, MODULATED[i] + 1)
                act.wait_ge(scaled, q + 1)
                if to_h:
                    dst = (hb[:, b, 1:1 + TP], hb[:, b, TP + 2:T + 2])
                else:
                    if b >= 2:
                        act.wait_ge(a_ready, BY[NORM_MOD[i][4]].a0 + b - 1)
                    dst = (work[:, 4 + b % 2, 0:TP], work[:, 4 + b % 2, TP:T])
                for z, cols in ((0, slice(0, TP)), (1, slice(TP, T))):
                    nc.scalar.activation(dst[z], work[:, 2 + b % 2, cols], ACT.Identity,
                                         bias=mod[:, sh + b, z:z + 1], scale=gs[:, b, z:z + 1]).then_inc(mod_done, 1)
                if not to_h:
                    act.wait_ge(mod_done, 2 * (q + 1))
                    nc.scalar.activation(ah[:, b, :], work[:, 4 + b % 2, :], ACT.Copy).then_inc(nhi_done, 1)

            def norm_pair(i):
                return lambda p: [modulate(i, b, False) for b in (2 * p, 2 * p + 1)]

            def mix_pair(i, before):
                def pair(p):
                    if before:
                        reader_done(act, BY[before], p)
                    for b in (2 * p, 2 * p + 1):
                        act.wait_ge(mix_ready, KB * (3 + i) + b + 1)
                        nc.scalar.activation(ah[:, b, :], work[:, b % 4, :], ACT.Copy).then_inc(mixhi_done, 1)
                return pair

            act.wait_ge(c_in, 16)
            nc.scalar.activation(cs[:], csg[:], ACT.Sigmoid).then_inc(c_sig, 1)
            act.wait_ge(eps_ready, 2)
            s = BY["ada0"]
            for j in range(8 + s.hoist):
                split(s, j)

            def body(it):
                for j in range(s.hoist, 8):
                    split(s, j, it)
                for j in range(s.hoist):
                    split(s, 8 + j, it)
            rounds(act, 1, 7, body)
            for j in range(s.hoist, 8):
                split(s, 56 + j)
            for j in range(BY["r"].hoist):
                split(BY["r"], j)
            norm_root(N_MIX0, x)
            for b in range(KB):
                modulate(N_MIX0, b, True)

            for i, f in enumerate((ACT.Tanh, ACT.Copy, ACT.Sigmoid)):
                act.wait_ge(mix_used, KB * (i + 1))
                for z in range(2 if i == 2 else 1):
                    m = 96 if i < 2 else P
                    nc.scalar.activation(mids[0:m, i + z, :], PS[0:m, i + z, 0:T], f).then_inc(mids_done, 1)

            gemm("r", "k", mix_pair(0, None))
            gemm("k", "v", mix_pair(1, "r"))
            gemm("v", None, mix_pair(2, "k"))

            def scan(it, h):
                lwn = f"lw{h}"
                for u in range(2):
                    t, m = lanes[u], L[u]
                    act.wait_ge(m["pre_mm"], 4 * it + Z)
                    nc.scalar.activation(t["t0"][:, 0:T], PS[:, 4 * u, 0:T], ACT.Sigmoid,
                                         bias=t[lwn][:, PW0:PW0 + 1]).then_inc(m["sg"], 1)
                    nc.scalar.activation(t["t1"][:, 0:T], PS[:, 4 * u + 1, 0:T], ACT.Sigmoid,
                                         bias=t[lwn][:, PA0:PA0 + 1]).then_inc(m["sg"], 1)
                    nc.scalar.activation(t["t2"][:], flat(k[:, bass.ds(2 * it + u, 1), :]), ACT.Square,
                                         scale=t[lwn][:, PKK:PKK + 1]).then_inc(m["sq"], 1)
                for u in range(2):
                    t, m = lanes[u], L[u]
                    act.wait_ge(m["cum"], it + 1)
                    cum = t["t3"][:].rearrange("p (c t) -> p c t", c=NCH)
                    nc.scalar.activation(t["e"][:, :, 1:C + 1], cum, ACT.Exp, scale=-DEC).then_inc(m["ex"], 1)
                    nc.scalar.activation(t["t4"][:], t["t3"][:], ACT.Exp, scale=DEC).then_inc(m["ex"], 1)
                for u in range(2):
                    t, m = lanes[u], L[u]
                    act.wait_ge(m["pre_mm"], 4 * it + SSQ)
                    nc.scalar.activation(t["t2"][:], PS[:, 4 * u + 2, 0:TT], ACT.Sqrt).then_inc(m["nrm"], 1)
                for u in range(2):
                    t, m = lanes[u], L[u]
                    act.wait_ge(m["prep"], it + 1)
                    nc.scalar.activation(t["t5"][:], flat(v[:, bass.ds(2 * it + u, 1), :]), ACT.Copy).then_inc(m["vc"], 1)
                for u in range(2):
                    t, m = lanes[u], L[u]
                    act.wait_ge(m["pre_mm"], 4 * it + TOK)
                    nc.scalar.activation(t["bk"][:, 0:4, :], PS[:, 4 * u, :].rearrange("p (c t) -> p c t", c=4),
                                         ACT.Copy).then_inc(m["tokc"], 1)
                    nc.scalar.activation(t["bk"][:, 4, :], PS[:, 4 * u + 1, 0:P], ACT.Copy).then_inc(m["tokc"], 1)
                    vps = PS[:, 4 * u + 2, 0:TT].rearrange("p (c t) -> p c t", c=NCH)
                    for n in ("sv", "uv"):
                        nc.scalar.activation(t[n][64:128, 0, :, :], vps[64:128], ACT.Copy).then_inc(m["tokc"], 1)
                        nc.scalar.activation(t[n][0:64, 1, :, :], vps[0:64], ACT.Copy).then_inc(m["tokc"], 1)
                for c in range(NCH):
                    for u in range(2):
                        t, m = lanes[u], L[u]
                        if c == NCH - 1:
                            act.wait_ge(m["s0"], 32 * it + 32)
                        if c:
                            act.wait_ge(m["sn"], 2 * NCH * it + 2 * c)
                        for z in range(2):
                            p = slice(64 * z, 64 * z + 64)
                            nc.scalar.activation(t["sd"][p, :], t["sv"][p, z, c, :], ACT.Copy,
                                                 scale=t["e"][p, c, C:C + 1]).then_inc(m["sd"], 1)
                    for u in range(2):
                        t, m = lanes[u], L[u]
                        act.wait_ge(m["u"], NCH * it + c + 1)
                        nc.scalar.activation(t["uv"][0:64, 0, c, :], PS[0:64, 4 * u + 1, 0:C], ACT.Copy).then_inc(m["uca"], 1)
                for u in range(2):
                    t, m = lanes[u], L[u]
                    act.wait_ge(m["post_mm"], 4 * it + Y)
                    nc.scalar.activation(t["t2"][0:64, :], PS[0:64, 4 * u, 0:TT], ACT.Copy).then_inc(m["yc"], 1)
                    nc.scalar.activation(t["t2"][64:128, :], PS[64:128, 4 * u + 1, 0:TT], ACT.Copy).then_inc(m["yc"], 1)
                for u in range(2):
                    t, m = lanes[u], L[u]
                    act.wait_ge(m["yd"], it + 1)
                    nc.scalar.activation(t["t3"][:], t["t2"][:], ACT.Square).then_inc(m["ys"], 1)
                for u in range(2):
                    t, m = lanes[u], L[u]
                    act.wait_ge(m["post_mm"], 4 * it + VAR)
                    nc.scalar.activation(t["t3"][:], PS[:, 4 * u + 3, 0:TT], ACT.Sqrt, bias=eps[:, 1:2]).then_inc(m["vs"], 1)
                for u in range(2):
                    t, m = lanes[u], L[u]
                    act.wait_ge(m["yg"], it + 1)
                    nc.scalar.activation(flat(ah[:, bass.ds(2 * it + u, 1), :]), t["t2"][:, 0:T], ACT.Copy).then_inc(m["oh"], 1)
            rounds(act, 0, KB // 4, lambda it: [scan(2 * it + h, h) for h in range(2)])

            for u in range(2):
                act.wait_ge(L[u]["free"], KB // 2 + 1)
                act.wait_ge(L[u]["sto"], 16 * (KB // 2))
            for j in range(BY["o"].hoist):
                split(BY["o"], j)
            gemm("o", "m1_0_0")
            norm_root(N_MLP0, x)
            for c in range(4):
                gemm(f"m1_0_{c}", f"m2_0_{c}", norm_pair(N_MLP0) if c == 0 else None)
                gemm(f"m2_0_{c}", f"m1_0_{c + 1}" if c < 3 else "kvd")

            norm_root(N_KV, x)
            s = BY["kvd"]
            for p in range(KB // 2):
                norm_pair(N_KV)(p)
                if p + s.hoist < s.per:
                    split(s, p + s.hoist)
            act.wait_ge(S["cache_in"], 16)
            nc.scalar.activation(kyh[:, :, TP:TP + PAST], cache[:, :, 0:PAST], ACT.Copy).then_inc(S["cachehi"], 1)
            for m in range(4):
                act.wait_ge(gemm_done, s.gd0 + m + 1)
                nc.scalar.activation(lat[:, m, 0:T], PS[:, m, 0:T], ACT.Copy).then_inc(bank_free[m], 1)
            for j in range(BY["wdq"].hoist):
                split(BY["wdq"], j)
            norm_root(N_LAT, lat)
            for m in range(4):
                act.wait_ge(S["lat_scaled"], m + 1)
                nc.scalar.activation(kyh[:, m, 0:TP], lat[:, m, 0:TP], ACT.Copy).then_inc(S["keys_hi"], 1)
                nc.scalar.activation(kyh[:, m, TP + PAST:KEYS], lat[:, m, TP:T], ACT.Copy).then_inc(S["keys_hi"], 1)
            norm_root(N_MIX1, x)
            act.wait_ge(slot_used, BY["wdq"].n0)
            s = BY["wdq"]
            for p in range(KB // 2):
                norm_pair(N_MIX1)(p)
                if p + s.hoist < s.per:
                    split(s, p + s.hoist)
            for j in range(BY["att0"].hoist):
                split(BY["att0"], j)
            for m in range(4):
                act.wait_ge(gemm_done, s.gd0 + m + 1)
                nc.scalar.activation(qn[:, m, :], PS[:, m, 0:T], ACT.Copy).then_inc(bank_free[m], 1)
            norm_root(N_Q, qn)
            for m in range(4):
                act.wait_ge(S["lat_scaled"], 4 + m + 1)
                nc.scalar.activation(cqh[:, m, :], qn[:, m, :], ACT.Copy).then_inc(S["cqhi"], 1)

            act.wait_ge(S["ckv_out"], 16)

            def out_hi(it, h, v4):
                act.wait_ge(S["o_acc"], v4 + h + 1)
                nc.scalar.activation(flat(ah[:, bass.ds(4 * it + h, 1), :]), PS[:, 4 + h, 0:T], ACT.Copy).then_inc(S["ohi"], 1)

            def group(s, g0, it, after):
                v1, v4 = it + (g0 + 1), it * 4 + 4 * g0
                for j in range(s.hoist, 6):
                    split(s, j, it)
                for m in range(4):
                    act.wait_ge(S["kt_acc"], v4 + m + 1)
                    nc.scalar.activation(kt[:, m, :], PS[:, m, 0:KEYS], ACT.Copy).then_inc(S["kt_done"], 1)
                for j in range(6, 8):
                    split(s, j, it)
                for m in range(4):
                    act.wait_ge(S["qn_acc"], v4 + m + 1)
                    nc.scalar.activation(qn[:, m, :], PS[:, m, 0:T], ACT.Copy).then_inc(S["qn_done"], 1)
                for j in range((after or s).hoist):
                    split(after or s, j if after else s.per + j, 0 if after else it)
                act.wait_ge(S["nmx"], v1)
                for h in range(4):
                    nc.scalar.activation(pr[:, h, 0:P], PS[:, 4 + h, 0:P], ACT.Exp, scale=SCALE,
                                         bias=mxs[:, h:h + 1], accum_out=sms[:, h:h + 1]).then_inc(S["ex"], 1)
                    nc.scalar.activation(pr[:, h, P:384], PS[:, 4 + h, P:384], ACT.Exp, scale=SCALE,
                                         bias=mxs[:, 4 + h:5 + h], accum_out=sms[:, 4 + h:5 + h]).then_inc(S["ex"], 1)
                nc.scalar.activation(prs[:], PS[:, 0, 0:SK], ACT.Exp, scale=SCALE,
                                     bias=mxs[:, 8:9], accum_out=sms[:, 8:9]).then_inc(S["ex"], 1)
                act.wait_ge(S["pts_acc"], v1)
                nc.scalar.activation(pts[:, 0, :], PS[:, 0, 0:P], ACT.Copy).then_inc(S["pts_done"], 1)
                nc.scalar.activation(pts[0:32, 1, :], PS[0:32, 0, P:2 * P], ACT.Copy).then_inc(S["pts_done"], 1)
                for h in range(4):
                    act.wait_ge(S["pt_acc"], v4 + h + 1)
                    if h >= 2:
                        act.wait_ge(S["o_acc"], v4 + h - 1)
                    nc.scalar.activation(pt[:, h % 2, :], PS[:, 1 + h % 2, 0:384], ACT.Copy).then_inc(S["pt_done"], 1)
                    if h >= 1:
                        out_hi(it, h - 1, v4)
                out_hi(it, 3, v4)

            for half in range(2):
                s = BY[f"att{half}"]
                rounds(act, 0, 3, lambda it: group(s, 4 * half, it, None))
                group(s, 4 * half, 3, BY[f"wo{half}"])
                gemm(f"wo{half}", "m1_1_0" if half else "att1")
            norm_root(N_MLP1, x)
            act.wait_ge(S["kpe_out"], 32)
            for c in range(4):
                gemm(f"m1_1_{c}", f"m2_1_{c}", norm_pair(N_MLP1) if c == 0 else None)
                gemm(f"m2_1_{c}", f"m1_1_{c + 1}" if c < 3 else None)
            norm_root(N_FIN, x)

        @block.vector
        def _(dve):
            ch = Count(dve, dve_chain)

            def split(s, j, it=0):
                n, step = s.n0 + j, it * s.per
                dve.wait_ge(hi_ready, step + (n + 1))
                if s.ada_slot(j):
                    nc.vector.memset(wlo[:, n % SPL, 0:1].bitcast(F32), 0.0).then_inc(lo_ready, 1)
                    return
                nc.vector.tensor_tensor(wlo[:, n % SPL, :], raw[:, n % RAW, :], whi[:, n % SPL, :],
                                        ALU.subtract).then_inc(lo_ready, 1)

            def row(s, it):
                g = s.ada0 + it
                used = s.n0 + (s.per - s.wide + 1)
                dve.wait_ge(slot_used, s.per * it + used)
                if s.name != "ada0" or not isinstance(it, int) or it:
                    dve.wait_ge(ada_fin, g)
                nc.vector.tensor_copy(arow[:], PS[:, 4, :]).then_inc(arow_ready, 1)

            def mods(g):
                dve.wait_ge(ada_fin, g + 1)
                nc.vector.tensor_tensor(mod[:, bass.ds(4 * g, 4), :],
                                        PS[:, 5, 0:8].rearrange("p (a t) -> p a t", a=4),
                                        vec[:, bass.ds(4 * g + ADAB, 4)].rearrange("p (a t) -> p a t", t=1).to_broadcast([P, 4, 2]),
                                        ALU.add).then_inc(mod_ready, 1)

            def epi(s, it, banks):
                if s.epi == "resid":
                    for m in banks:
                        bank_wait(dve, s, it, m)
                        for z, cols in ((0, slice(0, TP)), (1, slice(TP, T))):
                            xb = flat(x[:, bass.ds(4 * it + m, 1), cols])
                            ins = nc.vector.scalar_tensor_tensor(
                                out=xb, in0=PS[:, m, cols], scalar=flat(mod[:, bass.ds(4 * it + (KB * s.gate + m), 1), z:z + 1]),
                                in1=xb, op0=ALU.mult, op1=ALU.add)
                        ins.then_inc(bank_free[m], 1)
                elif s.epi == "relu2":
                    for m in banks:
                        i = s.hid0 + m
                        dve.wait_ge(bank_free[m], it + (s.free0[m] + 1))
                        nc.vector.tensor_tensor(work[:, 2 + m % 2, :], work[:, m % 2, :], work[:, m % 2, :],
                                                ALU.mult).then_inc(hid_sq, 1)
                        dve.wait_ge(hid_sq, 4 * it + (i + 1))
                        dve.wait_ge(sqhi_done, 4 * it + (i + 1))
                        nc.vector.tensor_tensor(flat(bl[:, bass.ds(4 * it + m, 1), :]), work[:, 2 + m % 2, :],
                                                flat(bh[:, bass.ds(4 * it + m, 1), :]), ALU.subtract).then_inc(b_ready, 1)

            def gemm(name, nxt, produce=None):
                walk(dve, BY[name], nxt, split, produce, epi, row, mods)

            def norm_scale(i):
                dve.wait_ge(root_done, i + 1)
                ch.inc(nc.vector.reciprocal(work[:, 6, :], work[:, 6, :]))
                if i in MODULATED:
                    _, sc, gain, need, _ = NORM_MOD[i]
                    dve.wait_ge(mod_ready, need)
                    if MODULATED[i]:
                        dve.wait_ge(mod_done, 2 * KB * MODULATED[i])
                    nc.vector.scalar_tensor_tensor(
                        out=gs[:], in0=mod[:, sc:sc + KB, :], scalar=1.0,
                        in1=vec[:, gain:gain + KB].rearrange("p (a t) -> p a t", t=1).to_broadcast([P, KB, 2]),
                        op0=ALU.add, op1=ALU.mult).then_inc(gs_done, 1)
                ch.wait()

            def scale_block(i, b):
                q = KB * MODULATED[i] + b
                if q >= 2:
                    dve.wait_ge(mod_done, 2 * (q - 1))
                nc.vector.tensor_tensor(work[:, 2 + b % 2, :], x[:, b, :], work[:, 6, :], ALU.mult).then_inc(scaled, 1)

            def norm_pair(i):
                def pair(p):
                    for b in ([0, 1] if p == 0 else []) + ([2 * p + 2, 2 * p + 3] if p < KB // 2 - 1 else []):
                        scale_block(i, b)
                    for b in (2 * p, 2 * p + 1):
                        dve.wait_ge(nhi_done, KB * (MODULATED[i] - 1) + b + 1)
                        nc.vector.tensor_tensor(al[:, b, :], work[:, 4 + b % 2, :], ah[:, b, :],
                                                ALU.subtract).then_inc(a_ready, 1)
                return pair

            def mix(col, q, b, place):
                dd = work[:, 4:6, :].rearrange("p a t -> p (a t)")
                if q:
                    dve.wait_ge(mix_ready, q)
                    ch.wait()
                ch.inc(nc.vector.tensor_tensor(dd[:, 0:T + 1], hb[:, b, 0:T + 1], hb[:, b, 1:T + 2], ALU.subtract))
                ch.wait()
                mu = vec[:, MU + KB * col + b:MU + KB * col + b + 1]
                for z, a, n in ((0, 0, TP), (1, TP + 1, TS)):
                    ins = nc.vector.scalar_tensor_tensor(out=work[:, place, a - z:a - z + n], in0=dd[:, a:a + n],
                                                         scalar=mu, in1=hb[:, b, a + 1:a + 1 + n],
                                                         op0=ALU.mult, op1=ALU.add)
                    if z:
                        ins.then_inc(mix_ready, 1)
                    else:
                        ch.inc(ins)

            def mix_pair(i, col, before):
                def pair(p):
                    for b in ([0, 1] if p == 0 else []) + ([2 * p + 2, 2 * p + 3] if p < KB // 2 - 1 else []):
                        q = KB * i + b
                        if q >= 4:
                            dve.wait_ge(mixhi_done, q - 3)
                            dve.wait_ge(a_ready, q - 3)
                        mix(col, KB * (3 + i) + b, b, b % 4)
                    if before:
                        reader_done(dve, BY[before], p)
                    for b in (2 * p, 2 * p + 1):
                        dve.wait_ge(mixhi_done, KB * i + b + 1)
                        nc.vector.tensor_tensor(al[:, b, :], work[:, b % 4, :], ah[:, b, :],
                                                ALU.subtract).then_inc(a_ready, 1)
                return pair

            nc.vector.memset(PS[:, 4, :], 0.0).then_inc(rows_zeroed, 1)
            nc.vector.memset(eps[:, 0:1], EPS).then_inc(eps_ready, 1)
            nc.vector.memset(eps[:, 1:2], GN_EPS).then_inc(eps_ready, 1)
            ch.inc(nc.vector.memset(hb[:, :, 0:1], 0.0))
            dve.wait_ge(vec_in, 16)
            dve.wait_ge(consts_in, 16)
            ch.inc(nc.vector.tensor_copy(hb[:, :, TP + 1:TP + 2], vec[:, SHIFT:SHIFT + KB].rearrange("p (a t) -> p a t", t=1)))
            dve.wait_ge(c_sig, 1)
            nc.vector.tensor_tensor(cs[:], cs[:], csg[:], ALU.mult).then_inc(silu_ready, 1)

            s = BY["ada0"]
            for j in range(8 + s.hoist):
                split(s, j)
                if j == 7:
                    row(s, 0)
            mods(0)

            def body(it):
                for j in range(s.hoist, 8):
                    split(s, j, it)
                row(s, it)
                for j in range(s.hoist):
                    split(s, 8 + j, it)
                mods(it)
            rounds(dve, 1, 7, body)
            for j in range(s.hoist, 8):
                split(s, 56 + j)
            row(s, 7)
            for j in range(BY["r"].hoist):
                split(BY["r"], j)
            mods(7)

            norm_scale(N_MIX0)
            for b in range(KB):
                scale_block(N_MIX0, b)
            dve.wait_ge(mod_done, 2 * KB)
            ch.inc(nc.vector.tensor_copy(last[:, 0, :], hb[:, :, TP:TP + 1].rearrange("p a t -> p (a t)")))
            ch.wait()
            nc.vector.tensor_copy(last[:, 1, :], hb[:, :, T + 1:T + 2].rearrange("p a t -> p (a t)")).then_inc(last_ready, 1)
            for i, col in enumerate((1, 4, 5)):
                for b in range(KB):
                    q = KB * i + b
                    if q >= 2:
                        dve.wait_ge(mix_used, q - 1)
                    mix(col, q, b, 2 + b % 2)
            dve.wait_ge(mix_used, 3 * KB)
            gemm("r", "k", mix_pair(0, 0, None))
            gemm("k", "v", mix_pair(1, 2, "r"))
            gemm("v", None, mix_pair(2, 3, "k"))

            for z in (r, k, v):
                ch.inc(nc.vector.memset(z[:, :, T:TT], 0.0))
            dve.wait_ge(slot_used, BY["o"].n0)
            dve.wait_ge(last_out, 16)
            for u in range(2):
                t, m = lanes[u], L[u]
                ch.inc(nc.vector.memset(t["t0"][:, T:TT], 0.0))
                ch.inc(nc.vector.memset(t["t1"][:, T:TT], 0.0))
                ch.inc(nc.vector.memset(t["e"][:, :, 0:1], 1.0))
                ch.inc(nc.vector.memset(t["sv"][0:64, 0, 0, :], 0.0))
                ch.inc(nc.vector.memset(t["sv"][64:128, 1, 0, :], 0.0))
                ch.wait()
                nc.vector.memset(t["w"][:], 0.0).then_inc(m["free"], 1)

            def scan(it, h):
                lwn = f"lw{h}"
                tt, stt = nc.vector.tensor_tensor, nc.vector.scalar_tensor_tensor

                def c3(ap):
                    return ap.rearrange("p (c t) -> p c t", c=NCH)

                def mask(col, p=slice(0, P)):
                    return con[p, col:col + C].rearrange("p (c t) -> p c t", c=1).to_broadcast([p.stop - p.start, NCH, C])

                top, bot = slice(0, 64), slice(64, 128)
                for u in range(2):
                    t, m = lanes[u], L[u]
                    dve.wait_ge(m["free"], it + 1)
                    ch.inc(nc.vector.memset(t["t0"][:, T:TT], 0.0))
                    ch.inc(nc.vector.memset(t["t1"][:, T:TT], 0.0))
                    ch.wait()
                    dve.wait_ge(m["sg"], 2 * it + 2)
                    nc.vector.tensor_tensor_scan(t["t3"][:], con[:, CARRY:CARRY + TT], t["t0"][:], 0.0,
                                                 ALU.mult, ALU.add).then_inc(m["cum"], 1)
                for u in range(2):
                    t, m = lanes[u], L[u]
                    lw = t[lwn]
                    rb, kb = (flat(z[:, bass.ds(2 * it + u, 1), :]) for z in (r, k))
                    eprev, enow = t["e"][:, :, 0:C], t["e"][:, :, 1:C + 1]
                    dve.wait_ge(m["sg"], 2 * it + 2)
                    dve.wait_ge(m["nrm"], it + 1)
                    ch.inc(nc.vector.tensor_scalar(t["t2"][:], t["t2"][:], 1e-12, None, ALU.max))
                    ch.inc(nc.vector.tensor_scalar(t["t5"][:], t["t1"][:], 1.0, lw[:, PKA:PKA + 1], ALU.subtract, ALU.mult))
                    ch.wait()
                    ch.inc(nc.vector.reciprocal(t["t2"][:], t["t2"][:]))
                    ch.wait()
                    ch.inc(stt(out=t["t2"][:], in0=kb, scalar=lw[:, PKK:PKK + 1], in1=t["t2"][:], op0=ALU.mult, op1=ALU.mult))
                    ch.wait()
                    ch.inc(stt(out=kb, in0=t["t5"][:], scalar=1.0, in1=kb, op0=ALU.add, op1=ALU.mult))
                    ch.inc(tt(t["t1"][:], t["t2"][:], t["t1"][:], ALU.mult))
                    dve.wait_ge(m["ex"], 2 * it + 2)
                    for z, p in ((0, top), (1, bot)):
                        ch.inc(stt(out=t["wl"][p, :, 2 * z, :], in0=c3(t["t2"][:])[p], scalar=-1.0, in1=eprev[p],
                                   op0=ALU.mult, op1=ALU.mult))
                    ch.wait()
                    ch.inc(stt(out=t["t0"][:], in0=rb, scalar=lw[:, PRK:PRK + 1], in1=kb, op0=ALU.mult, op1=ALU.mult))
                    for z, p in ((0, top), (1, bot)):
                        ch.inc(tt(t["bk"][p, :, C * z:C * z + C], c3(t["t1"][:])[p], c3(t["t4"][:])[p], ALU.mult))
                        ch.inc(tt(t["bk"][p, :, C - C * z:2 * C - C * z], c3(kb)[p], c3(t["t4"][:])[p], ALU.mult))
                    ch.wait()
                    tt(t["wl"][:, :, 1, :], c3(rb), enow, ALU.mult).then_inc(m["prep"], 1)
                for u in range(2):
                    t, m = lanes[u], L[u]
                    b0 = 4 * u
                    dve.wait_ge(m["pre_mm"], 4 * it + GRAM)
                    g = [flat(PS[:, b0 + 2 * z:b0 + 2 * z + 2, :])[:, 0:NCH * P].rearrange("p (c a t) -> p c a t", c=NCH, a=2)
                         for z in range(2)]
                    tt(t["nd"][top], g[0][top, :, 0], mask(MASK_S, top), ALU.mult).then_inc(m["masked"], 1)
                    tt(t["nd"][bot], g[1][bot, :, 1], mask(MASK_S, bot), ALU.mult).then_inc(m["masked"], 1)
                    tt(t["wl"][bot, :, 0, :], g[0][bot, :, 0], mask(MASK_S, bot), ALU.mult).then_inc(m["masked"], 1)
                    tt(t["wl"][top, :, 2, :], g[1][top, :, 1], mask(MASK_S, top), ALU.mult).then_inc(m["masked"], 1)
                    for z in range(2):
                        tt(t["gr"][:, z, :, :], g[z][:, :, 1 - z], mask(MASK_I), ALU.mult).then_inc(m["masked"], 1)
                for u in range(2):
                    t, m = lanes[u], L[u]
                    dve.wait_ge(m["pre_mm"], 4 * it + TOK)
                    tt(t["t0"][:], PS[:, 4 * u + 3, 0:TT], flat(v[:, bass.ds(2 * it + u, 1), :]), ALU.mult).then_inc(m["bv"], 1)
                for u in range(2):
                    t, m = lanes[u], L[u]
                    ch.inc(tt(c3(t["t5"][:]), t["nd"][:], mask(MASK_L), ALU.mult))
                    ch.wait()
                    tt(c3(t["t5"][:]), c3(t["t5"][:]), mask(EYE2), ALU.add).then_inc(m["xtu"], 1)
                for u in range(2):
                    t, m = lanes[u], L[u]
                    dve.wait_ge(m["q"], LEVELS * it + 1)
                    nc.vector.tensor_copy(t["t3"][:], PS[:, 4 * u, 0:TT]).then_inc(m["xu"], 1)
                for l in range(1, LEVELS):
                    for u in range(2):
                        t, m = lanes[u], L[u]
                        dve.wait_ge(m["q"], LEVELS * it + l + 1)
                        tt(c3(t["t4"][:]), c3(PS[:, 4 * u, 0:TT]), mask(MASK_L + C * l), ALU.mult).then_inc(m["qs"], 1)
                    for u in range(2):
                        t, m = lanes[u], L[u]
                        if l < LEVELS - 1:
                            dve.wait_ge(m["p1"], (LEVELS - 2) * it + l)
                            tt(t["t3"][:], PS[:, 4 * u + 1, 0:TT], t["t3"][:], ALU.add).then_inc(m["xu"], 1)
                    for u in range(2):
                        t, m = lanes[u], L[u]
                        dve.wait_ge(m["p2"], (LEVELS - 1) * it + l)
                        tt(t["t5"][:], PS[:, 4 * u + 2, 0:TT], t["t5"][:], ALU.add).then_inc(m["xtu"], 1)
                for c in range(NCH):
                    for u in range(2):
                        t, m = lanes[u], L[u]
                        dve.wait_ge(m["w"], NCH * it + c + 1)
                        nc.vector.tensor_copy(t["w"][:], PS[:, 4 * u, 0:C]).then_inc(m["wc"], 1)
                    for u in range(2):
                        t, m = lanes[u], L[u]
                        dve.wait_ge(m["u"], NCH * it + c + 1)
                        nc.vector.tensor_copy(t["uv"][bot, 1, c, :], PS[bot, 4 * u + 1, 0:C]).then_inc(m["ucd"], 1)
                    for u in range(2):
                        t, m = lanes[u], L[u]
                        dve.wait_ge(m["sp"], NCH * it + c + 1)
                        dve.wait_ge(m["sd"], 2 * NCH * it + 2 * c + 2)
                        for z, p in ((0, top), (1, bot)):
                            dst = t["sv"][p, z, c + 1, :] if c < NCH - 2 else t["st"][p, c - (NCH - 2), :]
                            stt(out=dst, in0=PS[p, 4 * u + 2, 0:C], scalar=t["e"][p, c, C:C + 1], in1=t["sd"][p, :],
                                op0=ALU.mult, op1=ALU.add).then_inc(m["sn"], 1)
                for u in range(2):
                    t, m = lanes[u], L[u]
                    dve.wait_ge(m["post_mm"], 4 * it + MEAN)
                    tt(t["t2"][:], t["t2"][:], PS[:, 4 * u + 2, 0:TT], ALU.subtract).then_inc(m["yd"], 1)
                for u in range(2):
                    t, m = lanes[u], L[u]
                    dve.wait_ge(m["vs"], it + 1)
                    ch.inc(nc.vector.reciprocal(t["t3"][:], t["t3"][:]))
                    dve.wait_ge(m["yd"], it + 1)
                    ch.wait()
                    ch.inc(tt(t["t2"][:], t["t2"][:], t["t3"][:], ALU.mult))
                    ch.wait()
                    ch.inc(nc.vector.tensor_scalar(t["t2"][:], t["t2"][:], t[lwn][:, PLG:PLG + 1], t[lwn][:, PLB:PLB + 1],
                                                   ALU.mult, ALU.add))
                    dve.wait_ge(m["bv"], it + 1)
                    ch.wait()
                    ch.inc(tt(t["t2"][:], t["t2"][:], t["t0"][:], ALU.add))
                    dve.wait_ge(m["post_mm"], 4 * it + GATE)
                    ch.wait()
                    tt(t["t2"][:, 0:T], t["t2"][:, 0:T], PS[:, 4 * u, 0:T], ALU.mult).then_inc(m["yg"], 1)
                for u in range(2):
                    t, m = lanes[u], L[u]
                    dve.wait_ge(m["yg"], it + 1)
                    dve.wait_ge(m["oh"], it + 1)
                    tt(flat(al[:, bass.ds(2 * it + u, 1), :]), t["t2"][:, 0:T],
                       flat(ah[:, bass.ds(2 * it + u, 1), :]), ALU.subtract).then_inc(a_ready, 1)
                    dve.wait_ge(m["sto"], 16 * it + 16)
                    dve.wait_ge(a_ready, 2 * it + (BY["o"].a0 + u + 1))
                    nc.vector.memset(t["t3"][:, 0:1], 0.0).then_inc(m["free"], 1)

            with dve.Fori(0, KB // 4) as it:
                ch.start(it, 2 * SCAN_CHAIN)
                for h in range(2):
                    scan(2 * it + h, h)
                ch.end(KB // 4)

            for u in range(2):
                dve.wait_ge(L[u]["free"], KB // 2 + 1)
            nc.vector.memset(PS[:, 4, :], 0.0).then_inc(rows_zeroed, 1)
            for j in range(BY["o"].hoist):
                split(BY["o"], j)
            dve.wait_ge(x_back, 16)
            gemm("o", "m1_0_0")
            norm_scale(N_MLP0)
            for c in range(4):
                gemm(f"m1_0_{c}", f"m2_0_{c}", norm_pair(N_MLP0) if c == 0 else None)
                gemm(f"m2_0_{c}", f"m1_0_{c + 1}" if c < 3 else "kvd")

            norm_scale(N_KV)
            s = BY["kvd"]
            for p in range(KB // 2):
                norm_pair(N_KV)(p)
                if p + s.hoist < s.per:
                    split(s, p + s.hoist)
            for j in range(BY["wdq"].hoist):
                split(BY["wdq"], j)
            dve.wait_ge(S["cachehi"], 1)
            nc.vector.tensor_tensor(kyl[:, :, TP:TP + PAST], cache[:, :, 0:PAST], kyh[:, :, TP:TP + PAST],
                                    ALU.subtract).then_inc(S["keys_ready"], 1)

            def rope(src, dst_parts, done):
                ch.inc(nc.vector.tensor_tensor(work[0:64, 4, :], src[0:64], trig[0:64, :], ALU.mult))
                ch.inc(nc.vector.tensor_tensor(work[0:64, 5, :], src[64:128], trig[64:128, :], ALU.mult))
                ch.wait()
                for dst, cols in dst_parts:
                    ins = nc.vector.tensor_tensor(dst, work[0:64, 4, cols], work[0:64, 5, cols], ALU.add)
                    ins.then_inc(done, 1)

            dve.wait_ge(S["trig_in"], 16)
            dve.wait_ge(gemm_done, s.gd0 + 5)
            rope(PS[:, 0, 0:T], ((kpe[0:64, 0:TP], slice(0, TP)), (kpe[0:64, TP + PAST:KEYS], slice(TP, T))), S["pe_done"])

            def latent_scale(i, src, gain, first):
                norm_scale(i)
                for m in range(4):
                    nc.vector.scalar_tensor_tensor(out=src[:, m, 0:T], in0=src[:, m, 0:T], scalar=vec[:, gain + m:gain + m + 1],
                                                   in1=work[:, 6, :], op0=ALU.mult, op1=ALU.mult).then_inc(S["lat_scaled"], 1)
                for m in range(4):
                    if first:
                        dve.wait_ge(S["lat_scaled"], m + 1)
                        dve.wait_ge(S["keys_hi"], 2 * m + 2)
                        for a, b in ((slice(0, TP), slice(0, TP)), (slice(TP + PAST, KEYS), slice(TP, T))):
                            nc.vector.tensor_tensor(kyl[:, m, a], src[:, m, b], kyh[:, m, a], ALU.subtract).then_inc(S["keys_ready"], 1)
                    else:
                        dve.wait_ge(S["lat_scaled"], 4 + m + 1)
                        dve.wait_ge(S["cqhi"], m + 1)
                        nc.vector.tensor_tensor(cql[:, m, :], src[:, m, :], cqh[:, m, :], ALU.subtract).then_inc(S["cq_ready"], 1)

            latent_scale(N_LAT, lat, LATG, True)
            norm_scale(N_MIX1)
            dve.wait_ge(slot_used, BY["wdq"].n0)
            s = BY["wdq"]
            for p in range(KB // 2):
                norm_pair(N_MIX1)(p)
                if p + s.hoist < s.per:
                    split(s, p + s.hoist)
            for j in range(BY["att0"].hoist):
                split(BY["att0"], j)
            latent_scale(N_Q, qn, QG, False)
            dve.wait_ge(S["ckv_out"], 16)
            dve.wait_ge(S["rows_in"], 96)

            def group(s, g0, it, after):
                v1, v4 = it + (g0 + 1), it * 4 + 4 * g0
                for j in range(s.hoist, 7):
                    split(s, j, it)
                for m in range(4):
                    n = P if m < 3 else TS
                    dve.wait_ge(S["v_acc"], v4 + m + 1)
                    nc.vector.tensor_copy(vt[0:n, m, :], PS[0:n, m, :]).then_inc(S["v_done"], 1)
                split(s, 7, it)
                for m in range(4):
                    dve.wait_ge(S["qr_acc"], v4 + m + 1)
                    rope(PS[:, m, 0:T], ((qp[0:64, m, :], slice(0, T)),), S["qr_done"])
                    dve.wait_ge(S["qr_done"], v4 + m + 1)
                for j in range((after or s).hoist):
                    split(after or s, j if after else s.per + j, 0 if after else it)
                dve.wait_ge(S["s_acc"], v1)
                ch.inc(nc.vector.tensor_reduce(mxs[:, 0:4], PS[:, 4:8, 0:P], AX.X, ALU.max))
                ch.inc(nc.vector.tensor_reduce(mxs[:, 4:8], PS[:, 4:8, P:384], AX.X, ALU.max))
                ch.inc(nc.vector.tensor_reduce(mxs[:, 8:9], PS[:, 0, 0:SK], AX.X, ALU.max))
                ch.wait()
                nc.vector.tensor_scalar(mxs[:], mxs[:], -SCALE, None, ALU.mult).then_inc(S["nmx"], 1)
                dve.wait_ge(S["ex"], 9 * v1)
                ch.inc(nc.vector.reciprocal(rsm[:], sms[:]))
                ch.wait()

                def bc(a, n, w):
                    return rsm[:, a:a + n].rearrange("p (a t) -> p a t", t=1).to_broadcast([P, n, w])

                nc.vector.tensor_scalar(prs[:], prs[:], rsm[:, 8:9], None, ALU.mult).then_inc(S["nrmd"], 1)
                nc.vector.tensor_tensor(pr[:, :, 0:P], pr[:, :, 0:P], bc(0, 4, P), ALU.mult).then_inc(S["nrmd"], 1)
                nc.vector.tensor_tensor(pr[:, :, P:384], pr[:, :, P:384], bc(4, 4, 2 * P), ALU.mult).then_inc(S["nrmd"], 1)
                for h in range(4):
                    dve.wait_ge(S["ohi"], v4 + h + 1)
                    nc.vector.tensor_tensor(flat(al[:, bass.ds(4 * it + h, 1), :]), PS[:, 4 + h, 0:T],
                                            flat(ah[:, bass.ds(4 * it + h, 1), :]), ALU.subtract).then_inc(a_ready, 1)

            per = 4 * 2 + 3 + 1
            for half in range(2):
                s = BY[f"att{half}"]
                with dve.Fori(0, 3) as it:
                    ch.start(it, per)
                    group(s, 4 * half, it, None)
                    ch.end(3)
                group(s, 4 * half, 3, BY[f"wo{half}"])
                gemm(f"wo{half}", "m1_1_0" if half else "att1")
            norm_scale(N_MLP1)
            dve.wait_ge(S["kpe_out"], 32)
            for c in range(4):
                gemm(f"m1_1_{c}", f"m2_1_{c}", norm_pair(N_MLP1) if c == 0 else None)
                gemm(f"m2_1_{c}", f"m1_1_{c + 1}" if c < 3 else None)
            norm_scale(N_FIN)
            for b in range(KB):
                nc.vector.scalar_tensor_tensor(out=x[:, b, :], in0=x[:, b, :], scalar=vec[:, G_FIN + b:G_FIN + b + 1],
                                               in1=work[:, 6, :], op0=ALU.mult, op1=ALU.mult).then_inc(y_ready, 1)

        @block.tensor
        def _(pe):
            mm = nc.tensor.matmul

            def ada_slot(s, it, p, n, first):
                pe.wait_ge(lo_ready, s.per * it + (n + 1))
                if p == 0 and not first:
                    pe.wait_ge(arow_ready, s.ada0 + it)
                for j in range(2):
                    for z in range(2):
                        g, a = 64 * j + 32 * z, 256 * z
                        ins = mm(PS[g:g + 2, 4, a:a + 256], cs[:, 2 * p + j, :],
                                 wf[:, n % SPL, 512 * j + a:512 * j + a + 256], start=p == 0, stop=p == 7)
                ins.then_inc(slot_used, 1)

            def ada_finish(g, first=False):
                pe.wait_ge(arow_ready, g + 1)
                if not first:
                    pe.wait_ge(mod_ready, g)
                for m in range(4):
                    ins = mm(PS[:, 5, 2 * m:2 * m + 2], arow[:, P * m:P * m + P], con[:, SEL:SEL + 2],
                             start=True, stop=True)
                ins.then_inc(ada_fin, 1)

            def three(out, wh, wl, xh, xl, start, stop):
                mm(out, wh, xh, start=start, stop=False)
                mm(out, wl, xh, start=False, stop=False)
                return mm(out, wh, xl, start=False, stop=stop)

            def gemm_slot(s, it, p, n, xh, xl):
                pe.wait_ge(lo_ready, s.per * it + (n + 1))
                if s.src == "A":
                    pe.wait_ge(a_ready, s.a0 + 2 * p + 2)
                else:
                    pe.wait_ge(b_ready, s.hid0 + 2 * p + 2)
                for m in range(4):
                    if p == 0:
                        if s.free0[m] or not isinstance(it, int):
                            pe.wait_ge(bank_free[m], it + s.free0[m])
                    for j in range(2):
                        a = 512 * j + P * m
                        ins = three(PS[:, m, 0:T], whi[:, n % SPL, a:a + P], wlo[:, n % SPL, a:a + P],
                                    xh[:, 2 * p + j, :], xl[:, 2 * p + j, :], p == 0 and j == 0, p == 7 and j == 1)
                    if p == 7 and m < 3:
                        ins.then_inc(gemm_done, 1)
                ins.then_inc(slot_used, 1)

            def gemm(name):
                s = BY[name]
                xh, xl = (ah, al) if s.src == "A" else (bh, bl)

                def group(it):
                    for p in range(8):
                        n = s.n0 + s.wide * p
                        if s.mixed:
                            ada_slot(s, it, p, n, False)
                            n += 1
                        gemm_slot(s, it, p, n, xh, xl)
                    if s.mixed:
                        ada_finish(s.ada0 + it)
                if name == "r":
                    group(0)
                    rounds(pe, 1, 4, group)
                else:
                    rounds(pe, 0, 4, group)

            def mean_square(i, ones):
                for b in range(NORMS[i][0]):
                    pe.wait_ge(sq_ready, SQ0[i] + b + 1)
                    mm(PS[:, 6, 0:T], con[:, ones:ones + P], work[:, b % 2, :], start=b == 0,
                       stop=b == NORMS[i][0] - 1).then_inc(sq_used, 1)

            pe.wait_ge(silu_ready, 1)
            pe.wait_ge(rows_zeroed, 1)
            pe.wait_ge(consts_in, 16)
            s = BY["ada0"]
            for p in range(8):
                ada_slot(s, 0, p, p, True)
            ada_finish(0, True)

            def body(it):
                for p in range(8):
                    ada_slot(s, it, p, p, False)
                ada_finish(it)
            rounds(pe, 1, 8, body)
            mean_square(N_MIX0, ONES_D)

            pe.wait_ge(lora1_in, 48)
            for i, (w, parts) in enumerate(((l1w, 1), (l1a, 1), (l1g, 2))):
                m = 96 if i < 2 else P
                for b in range(KB):
                    pe.wait_ge(mix_ready, KB * i + b + 1)
                    for z in range(parts):
                        ins = mm(PS[0:m, i + z, 0:T], w[:, b, P * z:P * z + m], work[:, 2 + b % 2, :],
                                 start=b == 0, stop=b == KB - 1)
                    ins.then_inc(mix_used, 1)
            pe.wait_ge(mids_done, 4)
            gemm("r")
            gemm("k")
            gemm("v")

            pe.wait_ge(bank_free[3], BY["o"].free0[3])

            def scan(it, h, rnd):
                lwn = f"lw{h}"
                top, bot = slice(0, 64), slice(64, 128)
                for u in range(2):
                    t, m = lanes[u], L[u]
                    b0 = 4 * u
                    pe.wait_ge(m["free"], it + 1)
                    pe.wait_ge(m[lwn], 16 * rnd + 16)
                    mm(PS[:, b0, 0:T], t[lwn][0:96, LW_W:LW_W + P], mids[0:96, 0, :], start=True, stop=True)
                    mm(PS[:, b0 + 1, 0:T], t[lwn][0:96, LW_A:LW_A + P], mids[0:96, 1, :], start=True,
                       stop=True).then_inc(m["pre_mm"], 1)
                for u in range(2):
                    t, m = lanes[u], L[u]
                    pe.wait_ge(m["sq"], it + 1)
                    mm(PS[:, 4 * u + 2, 0:TT], con[:, BD1:BD1 + P], t["t2"][:], start=True, stop=True).then_inc(m["pre_mm"], 1)
                for u in range(2):
                    t, m = lanes[u], L[u]
                    b0 = 4 * u
                    pe.wait_ge(m["prep"], it + 1)
                    for c in range(NCH):
                        for z, p in ((0, top), (1, bot)):
                            ins = mm(PS[:, b0 + 2 * z + c // 4, P * (c % 4):P * (c % 4) + P], t["bk"][p, c, :],
                                     t["wl"][p, c, z:z + 2, :], start=True, stop=True)
                    ins.then_inc(m["pre_mm"], 1)
                for u in range(2):
                    t, m = lanes[u], L[u]
                    b0 = 4 * u
                    pe.wait_ge(m["masked"], 6 * it + 6)
                    pe.wait_ge(m["vc"], it + 1)
                    for c in range(NCH):
                        nc.tensor.transpose(PS[:, b0 + c // 4, P * (c % 4):P * (c % 4) + P], t["bk"][:, c, :], ident)
                    for c in range(NCH):
                        tok = slice(C * c, C * c + C)
                        mm(PS[64:128, b0 + 2, tok], t["t5"][:, tok], con[:, IDENT:IDENT + C], start=True, stop=True)
                        mm(PS[0:64, b0 + 2, tok], t["t5"][:, tok], con[:, IDENT + C:IDENT + P], start=True, stop=True)
                    mm(PS[:, b0 + 3, 0:TT], con[:, BD1:BD1 + P], t["t0"][:], start=True, stop=True).then_inc(m["pre_mm"], 1)
                def by_head(u, bank, lhs, rhs):
                    pe.sem_inc(quarters, 1)
                    for c in range(NCH):
                        tok = slice(C * c, C * c + C)
                        for p in (top, bot):
                            ins = mm(PS[p, 4 * u + bank, tok], lhs[p, tok], rhs(p, tok), start=True, stop=True)
                    return ins

                for u in range(2):
                    t, m = lanes[u], L[u]
                    pe.wait_ge(m["tokc"], 6 * it + 6)
                    pe.wait_ge(m["xtu"], LEVELS * it + 1)
                    by_head(u, 0, t["t5"], lambda p, tok: con[p, EYE2:EYE2 + C]).then_inc(m["q"], 1)
                for l in range(1, LEVELS):
                    for u in range(2):
                        t, m = lanes[u], L[u]
                        pe.wait_ge(m["xu"], (LEVELS - 1) * it + l)
                        by_head(u, 0, flat(t["nd"][:]), lambda p, tok: t["t3"][p, tok]).then_inc(m["q"], 1)
                    for u in range(2):
                        t, m = lanes[u], L[u]
                        pe.wait_ge(m["xtu"], LEVELS * it + l)
                        pe.wait_ge(m["qs"], (LEVELS - 1) * it + l)
                        if l < LEVELS - 1:
                            by_head(u, 1, t["t5"], lambda p, tok: t["t4"][p, tok]).then_inc(m["p1"], 1)
                    for u in range(2):
                        t, m = lanes[u], L[u]
                        by_head(u, 2, t["t4"], lambda p, tok: t["t5"][p, tok]).then_inc(m["p2"], 1)
                for c in range(NCH):
                    tok = slice(C * c, C * c + C)
                    for u in range(2):
                        t, m = lanes[u], L[u]
                        b0 = 4 * u
                        if c == 0:
                            pe.wait_ge(m["xtu"], LEVELS * it + LEVELS)
                            pe.wait_ge(m["bv"], it + 1)
                        elif c < NCH - 1:
                            pe.wait_ge(m["sn"], 2 * NCH * it + 2 * c)
                        else:
                            pe.wait_ge(m["s0"], 32 * it + 32)
                            pe.wait_ge(m["wc"], NCH * it + c)
                        mm(PS[0:64, b0, 0:C], t["wl"][:, c, 0, :], t["sv"][:, 0, c, :], start=True, stop=True)
                        mm(PS[64:128, b0, 0:C], t["wl"][:, c, 2, :], t["sv"][:, 1, c, :], start=True,
                           stop=True).then_inc(m["w"], 1)
                    for u in range(2):
                        t, m = lanes[u], L[u]
                        b0 = 4 * u
                        pe.wait_ge(m["wc"], NCH * it + c + 1)
                        if c:
                            pe.wait_ge(m["uca"], NCH * it + c)
                            pe.wait_ge(m["ucd"], NCH * it + c)
                        pe.sem_inc(quarters, 1)
                        mm(PS[0:64, b0 + 1, 0:C], t["t5"][top, tok], t["w"][top], start=True, stop=True)
                        mm(PS[64:128, b0 + 1, 0:C], t["t5"][bot, tok], t["w"][bot], start=True, stop=True).then_inc(m["u"], 1)
                    for u in range(2):
                        t, m = lanes[u], L[u]
                        b0 = 4 * u
                        pe.wait_ge(m["uca"], NCH * it + c + 1)
                        pe.wait_ge(m["ucd"], NCH * it + c + 1)
                        if c:
                            pe.wait_ge(m["sn"], 2 * NCH * it + 2 * c)
                        mm(PS[0:64, b0 + 2, 0:C], t["bk"][:, c, 0:C], t["uv"][:, 0, c, :], start=True, stop=True)
                        mm(PS[64:128, b0 + 2, 0:C], t["bk"][:, c, C:P], t["uv"][:, 1, c, :], start=True,
                           stop=True).then_inc(m["sp"], 1)
                for u in range(2):
                    t, m = lanes[u], L[u]
                    b0 = 4 * u
                    for z, p in ((0, top), (1, bot)):
                        for c in range(NCH):
                            tok = slice(C * c, C * c + C)
                            mm(PS[p, b0 + z, tok], t["sv"][p, z, c, :], t["wl"][p, c, 1, :], start=True, stop=False)
                            ins = mm(PS[p, b0 + z, tok], t["uv"][:, z, c, :], t["gr"][:, z, c, :], start=False, stop=True)
                    ins.then_inc(m["post_mm"], 1)
                for u in range(2):
                    t, m = lanes[u], L[u]
                    pe.wait_ge(m["yc"], 2 * it + 2)
                    pe.wait_ge(m["sn"], 2 * NCH * it + 2 * NCH)
                    mm(PS[:, 4 * u + 2, 0:TT], con[:, BD64:BD64 + P], t["t2"][:], start=True, stop=True).then_inc(m["post_mm"], 1)
                for u in range(2):
                    t, m = lanes[u], L[u]
                    pe.wait_ge(m["ys"], it + 1)
                    mm(PS[:, 4 * u + 3, 0:TT], con[:, BD64:BD64 + P], t["t3"][:], start=True, stop=True).then_inc(m["post_mm"], 1)
                for u in range(2):
                    t, m = lanes[u], L[u]
                    mm(PS[:, 4 * u, 0:T], t[lwn][:, LW_G:LW_G + P], mids[:, 2, :], start=True, stop=False)
                    mm(PS[:, 4 * u, 0:T], t[lwn][:, LW_G + P:LW_G + 2 * P], mids[:, 3, :], start=False,
                       stop=True).then_inc(m["post_mm"], 1)
            rounds(pe, 0, KB // 4, lambda it: [scan(2 * it + h, h, it) for h in range(2)])
            for u in range(2):
                pe.wait_ge(L[u]["free"], KB // 2 + 1)
            pe.wait_ge(rows_zeroed, 2)
            gemm("o")
            mean_square(N_MLP0, ONES_D)
            for c in range(4):
                gemm(f"m1_0_{c}")
                gemm(f"m2_0_{c}")
            mean_square(N_KV, ONES_D)

            def four(s, xh, xl, acc):
                for p in range(8):
                    n = s.n0 + p
                    pe.wait_ge(lo_ready, n + 1)
                    pe.wait_ge(a_ready, s.a0 + 2 * p + 2)
                    for m in range(4):
                        if p == 0:
                            pe.wait_ge(bank_free[m], s.free0[m])
                        for j in range(2):
                            a = 512 * j + P * m
                            ins = three(PS[:, m, 0:T], whi[:, n % SPL, a:a + P], wlo[:, n % SPL, a:a + P],
                                        xh[:, 2 * p + j, :], xl[:, 2 * p + j, :], p == 0 and j == 0, p == 7 and j == 1)
                        if p == 7:
                            ins.then_inc(acc, 1)
                    if p < 7:
                        ins.then_inc(slot_used, 1)
            s = BY["kvd"]
            four(s, ah, al, gemm_done)
            pe.wait_ge(gemm_done, s.gd0 + 4)
            pe.sem_inc(slot_used, 1)
            pe.wait_ge(bank_free[0], s.free0[0] + 1)
            for q in range(2):
                n = s.n0 + 8 + q
                pe.wait_ge(lo_ready, n + 1)
                for j in range(8):
                    b = 8 * q + j
                    ins = three(PS[:, 0, 0:T], whi[:, n % SPL, P * j:P * j + P], wlo[:, n % SPL, P * j:P * j + P],
                                ah[:, b, :], al[:, b, :], b == 0, b == KB - 1)
                ins.then_inc(gemm_done if q else slot_used, 1)
            pe.wait_ge(gemm_done, s.gd0 + 5)
            pe.sem_inc(slot_used, 1)
            mean_square(N_LAT, ONES_Q)
            mean_square(N_MIX1, ONES_D)
            pe.wait_ge(S["pe_done"], 2)
            s = BY["wdq"]
            four(s, ah, al, gemm_done)
            pe.wait_ge(gemm_done, s.gd0 + 4)
            pe.sem_inc(slot_used, 1)
            mean_square(N_Q, ONES_Q)
            pe.wait_ge(S["rows_in"], 96)
            pe.wait_ge(S["keys_ready"], 9)
            pe.wait_ge(S["cq_ready"], 4)
            pe.wait_ge(S["pe_done"], 2)
            for m in range(4):
                pe.wait_ge(bank_free[m], BY["wdq"].free0[m] + 1)

            def project(s, it, q0, acc, v4, width, xh, xl, wait):
                for q in range(2):
                    n = s.n0 + q0 + q
                    pe.wait_ge(lo_ready, s.per * it + (n + 1))
                    for m in range(4):
                        if q == 0:
                            wait(m)
                        for j in range(2):
                            a = 512 * j + P * m
                            ins = three(PS[:, m, 0:width], whi[:, n % SPL, a:a + P], wlo[:, n % SPL, a:a + P],
                                        xh[:, 2 * q + j, :], xl[:, 2 * q + j, :], q == 0 and j == 0, q == 1 and j == 1)
                        if q == 1:
                            ins.then_inc(acc, 1)
                    if q == 0:
                        ins.then_inc(slot_used, 1)
                pe.wait_ge(acc, v4 + 4)
                pe.sem_inc(slot_used, 1)

            def group(s, g0, it):
                v1, v4 = it + (g0 + 1), it * 4 + 4 * g0

                def after_group(m):
                    if g0 == 0 and isinstance(it, int) and it == 0:
                        return
                    if m == 0:
                        pe.wait_ge(S["pts_done"], 2 * it + 2 * g0)
                    elif m < 3:
                        pe.wait_ge(S["pt_done"], v4)
                    if g0 == 4:
                        pe.wait_ge(bank_free[m], s.free0[m])
                project(s, it, 0, S["kt_acc"], v4, KEYS, kyh, kyl, after_group)
                for q in range(2):
                    n = s.n0 + 2 + q
                    pe.wait_ge(lo_ready, s.per * it + (n + 1))
                    for m in range(4):
                        w = P if m < 3 else TS
                        if q == 0:
                            pe.wait_ge(S["kt_done"], v4 + m + 1)
                        for j in range(2):
                            cols = slice(P * m, P * m + w)
                            kb = 2 * q + j
                            o, wa = PS[0:w, m, :], slice(512 * j, 512 * j + 512)
                            mm(o, kyh[:, kb, cols], whi[:, n % SPL, wa], start=kb == 0, stop=False)
                            mm(o, kyl[:, kb, cols], whi[:, n % SPL, wa], start=False, stop=False)
                            ins = mm(o, kyh[:, kb, cols], wlo[:, n % SPL, wa], start=False, stop=kb == 3)
                        if q == 1:
                            ins.then_inc(S["v_acc"], 1)
                    if q == 0:
                        ins.then_inc(slot_used, 1)
                pe.wait_ge(S["v_acc"], v4 + 4)
                pe.sem_inc(slot_used, 1)
                project(s, it, 4, S["qn_acc"], v4, T, cqh, cql, lambda m: pe.wait_ge(S["v_done"], v4 + m + 1))
                project(s, it, 6, S["qr_acc"], v4, T, cqh, cql, lambda m: pe.wait_ge(S["qn_done"], v4 + m + 1))
                for h in range(4):
                    pe.wait_ge(S["qr_done"], v4 + h + 1)
                    for a, b, qc, kc in ((0, P, slice(0, P), slice(0, P)), (P, 384, slice(P, TP), slice(0, TP))):
                        mm(PS[:, 4 + h, a:b], qn[:, h, qc], kt[:, h, kc], start=True, stop=False)
                        mm(PS[:, 4 + h, a:b], qp[0:66, h, qc], kpe[0:66, kc], start=False, stop=True)
                for h in range(4):
                    if h == 0:
                        pe.wait_ge(S["qr_done"], v4 + 4)
                    o = PS[32 * h:32 * h + 32, 0, 0:SK]
                    mm(o, qn[:, h, TP:T], kt[:, h, TP:KEYS], start=True, stop=False)
                    ins = mm(o, qp[0:66, h, TP:T], kpe[0:66, TP:KEYS], start=False, stop=True)
                ins.then_inc(S["s_acc"], 1)
                pe.wait_ge(S["nrmd"], 3 * v1 - 2)
                nc.tensor.transpose(PS[:, 0, 0:P], prs[:, 0:P], ident)
                nc.tensor.transpose(PS[0:32, 0, P:2 * P], prs[:, P:SK], ident).then_inc(S["pts_acc"], 1)
                pe.wait_ge(S["nrmd"], 3 * v1)

                def turn(h):
                    if h >= 2:
                        pe.wait_ge(S["pt_done"], v4 + h - 1)
                    for c in range(3):
                        ins = nc.tensor.transpose(PS[:, 1 + h % 2, P * c:P * c + P], pr[:, h, P * c:P * c + P], ident)
                    ins.then_inc(S["pt_acc"], 1)

                def values(h):
                    hd = slice(P * h, P * h + P)
                    pe.wait_ge(S["pt_done"], v4 + h + 1)
                    if h == 0:
                        pe.wait_ge(S["pts_done"], 2 * v1)
                    mm(PS[:, 4 + h, 0:TP], vt[:, 0, hd], pt[:, h % 2, 0:TP], start=True, stop=False)
                    mm(PS[:, 4 + h, P:TP], vt[:, 1, hd], pt[:, h % 2, TP:384], start=False, stop=True)
                    mm(PS[:, 4 + h, TP:T], vt[:, 2, hd], pts[:, 0, 32 * h:32 * h + 32], start=True, stop=False)
                    mm(PS[:, 4 + h, TP:T], vt[0:32, 3, hd], pts[0:32, 1, 32 * h:32 * h + 32], start=False,
                       stop=True).then_inc(S["o_acc"], 1)
                turn(0)
                turn(1)
                for h in range(4):
                    values(h)
                    if h < 2:
                        turn(h + 2)

            for half in range(2):
                s = BY[f"att{half}"]
                if half == 0:
                    group(s, 0, 0)
                rounds(pe, 1 - half, 4, lambda it: group(s, 4 * half, it))
                pe.wait_ge(S["pts_done"], 8 * half + 8)
                pe.wait_ge(S["pt_done"], 16 * half + 16)
                gemm(f"wo{half}")
            mean_square(N_MLP1, ONES_D)
            for c in range(4):
                gemm(f"m1_1_{c}")
                gemm(f"m2_1_{c}")
            mean_square(N_FIN, ONES_D)


def halves(w):
    kk, m = w.shape
    a = w.reshape(kk // 256, 2, P, m // 512, 512).transpose(3, 0, 2, 1, 4)
    return a.reshape(-1, P, HS)


def woven(a, b):
    return np.stack([a, b], 1).reshape(-1, P, HS)


def column(a):
    return np.asarray(a).reshape(-1, P).T


def tokens(p, s):
    a = np.concatenate([p, s], 0)
    return np.ascontiguousarray(a.T.reshape(-1, P, a.shape[0]).transpose(1, 0, 2))


def constants():
    c = np.zeros((P, NCONST), np.float32)
    p, t = np.arange(P)[:, None], np.arange(C)[None, :]
    c[:, IDENT:IDENT + P] = np.eye(P)
    c[:, ONES_D:ONES_D + P] = 1.0 / D
    c[:, ONES_Q:ONES_Q + P] = 1.0 / KV
    same = (p // C) == (np.arange(P)[None, :] // C)
    c[:, BD1:BD1 + P] = same
    c[:, BD64:BD64 + P] = same / C
    i = p % C
    c[:, MASK_S:MASK_S + C] = i < t
    c[:, MASK_I:MASK_I + C] = i <= t
    for l in range(LEVELS):
        joined = ((i >> (l + 1)) == (t >> (l + 1))) & ((i >> l) % 2 == 1) & ((t >> l) % 2 == 0)
        c[:, MASK_L + C * l:MASK_L + C * l + C] = joined
    c[:, MASK_L:MASK_L + C] = (i // 2 == t // 2) & (i % 2 == 0) & (t % 2 == 1)
    c[:, EYE2:EYE2 + C] = i == t
    c[:, CARRY:CARRY + TT] = np.arange(TT)[None, :] % C != 0
    for q in range(0, P, 32):
        c[q, SEL] = c[q + 1, SEL + 1] = 1.0
    return c


def rotary():
    half = ROPE // 2
    inv = np.float32(10000.0) ** (-np.arange(half, dtype=np.float32) / np.float32(half))
    pos = np.concatenate([np.arange(TP), PAST + np.arange(TS)]).astype(np.float32)
    ang = (inv[:, None] * pos[None, :]).astype(np.float32)
    cos, sin = np.cos(ang), np.sin(ang)
    return np.concatenate([cos, cos, -sin, sin], 0).astype(np.float32)


def swapped(w):
    return np.concatenate([w, w[..., ROPE // 2:], w[..., :ROPE // 2]], -1)


def kernel(**inputs):
    import concourse.bacc as bacc
    from concourse.bass_utils import run_bass_kernel_spmd

    a = {n: np.asarray(z) for n, z in inputs.items()}
    f = np.float32
    ada = [a["ada_w"][0], a["ada_w"][1], a["kv_ada_w"]]
    own = halves(ada[0])
    later = np.concatenate([halves(ada[1]), halves(ada[2])], 0)
    parts = [own[:64]]
    for i, n in enumerate(("rw_wr", "rw_wk", "rw_wv", "rw_wo")):
        parts.append(woven(own[64 + 32 * i:96 + 32 * i], halves(a[n][0])))
    for layer in range(2):
        for c in range(4):
            cols = slice(D * c, D * c + D)
            for j, w in enumerate((a["mlp_w1"][layer][:, cols], a["mlp_w2"][layer][cols])):
                h = halves(w)
                g = 32 * (2 * c + j)
                parts.append(woven(later[g:g + 32], h) if layer == 0 else h)
        if layer:
            break
        parts.append(halves(a["kv_wd"][:, :KV]))
        pe = swapped(a["kv_wd"][:, KV:])
        parts.append(pe.reshape(2, 8, P, P).transpose(0, 2, 1, 3).reshape(2, P, HS))
        parts.append(halves(a["mla_wdq"][0]))
        wq = a["mla_wuq"][0].reshape(KV, HEADS, NOPE + ROPE)
        per = [halves(a["kv_wuk"].reshape(KV, -1)), halves(a["kv_wuv"].reshape(KV, -1)),
               halves(np.ascontiguousarray(wq[..., :NOPE]).reshape(KV, -1)), halves(swapped(wq[..., NOPE:]).reshape(KV, -1))]
        per = np.stack([z.reshape(8, 2, P, HS) for z in per], 1).reshape(8, 8, P, HS)
        for half in range(2):
            parts.append(per[4 * half:4 * half + 4].reshape(-1, P, HS))
            parts.append(halves(a["mla_wo"][0][D * half:D * half + D]))
    stream = np.concatenate(parts, 0)

    vec = np.concatenate([column(z) for z in (
        a["ada_b"][0], a["ada_b"][1], a["kv_ada_b"], a["norm_mix_g"][0], a["norm_mlp_g"][0], a["norm_mix_g"][1],
        a["norm_mlp_g"][1], a["kv_norm_g"], a["final_g"], a["rw_mu"][0].reshape(-1), a["state_shift"][0, 0],
        a["kv_lat_g"], a["mla_q_g"][0])], 1)
    lw = np.zeros((KB, P, NLW), f)
    for i, w in enumerate((a["rw_w2"][0], a["rw_a2"][0])):
        lw[:, 0:96, P * i:P * i + P] = w.reshape(96, KB, P).transpose(1, 0, 2)
    g2 = a["rw_g2"][0].reshape(2, P, KB, P)
    for i in range(2):
        lw[:, :, LW_G + P * i:LW_G + P * i + P] = g2[i].transpose(1, 0, 2)
    for i, n in enumerate(("rw_w0", "rw_a0", "rw_kk", "rw_ka", "rw_rk", "rw_lnx_g", "rw_lnx_b")):
        lw[:, :, LW_P + i] = a[n][0].reshape(KB, P)
    s0 = a["state_wkv"][0, 0].transpose(0, 2, 1).reshape(KB, P, C)
    krow = np.zeros((2, KEYS), f)
    qrow = np.zeros((2, T), f)
    for i in range(2):
        krow[i, P * i + C:P * i + 2 * C] = -1e30
        qrow[i, P * i:P * i + C] = 1.0

    ins = {
        "stream": stream, "xT": tokens(a["x_prompt"][0], a["x_sample"][0]),
        "cT": np.stack([column(a["c_prompt"][0]), column(a["c_sample"][0])], -1),
        "con": constants(), "vec": vec, "lw": lw, "s0": s0,
        "l1w": a["rw_w1"][0].reshape(KB, P, 96).transpose(1, 0, 2),
        "l1a": a["rw_a1"][0].reshape(KB, P, 96).transpose(1, 0, 2),
        "l1g": a["rw_g1"][0].reshape(KB, P, 256).transpose(1, 0, 2),
        "trig": rotary(), "krow": krow, "qrow": qrow,
        "cckv": a["cache_ckv"][0].T.reshape(4, P, PAST).transpose(1, 0, 2), "ckpe": a["cache_kpe"][0].T,
    }
    outs = {"yT": (P, KB, T), "ckvT": (P, 4, T), "kpeT": (ROPE, T), "wkvT": (KB, P, 2, C), "shiftT": (P, 2, KB)}
    nc = bacc.Bacc("TRN2", target_bir_lowering=False, num_devices=1)
    d = {}
    for n in ins:
        ins[n] = np.ascontiguousarray(ins[n])
        d[n] = nc.dram_tensor(n, ins[n].shape, F32, kind="ExternalInput").ap()
    for n, shape in outs.items():
        d[n] = nc.dram_tensor(n, shape, F32, kind="ExternalOutput").ap()
    trunk(nc, d)
    got = run_bass_kernel_spmd(nc, [ins], core_ids=[0]).results[0]

    def rows(z, n):
        return z.transpose(2, 1, 0).reshape(T, n * P)

    y, ckv, kpe = rows(got["yT"], KB), rows(got["ckvT"], 4), got["kpeT"].T
    wkv = got["wkvT"].reshape(KB, 2, C, 2, C).transpose(3, 0, 1, 4, 2).reshape(2, 1, 1, HEADS, C, C)
    shift = got["shiftT"].transpose(1, 2, 0).reshape(2, 1, 1, D)
    return tuple(np.ascontiguousarray(z) for z in (
        y[None, :TP], y[None, TP:], ckv[None, :TP], kpe[None, :TP], wkv[0], shift[0],
        ckv[None, TP:], kpe[None, TP:], wkv[1], shift[1]))
```
